# Optimizing a Trainium2 kernel written in Bass

```python
import math
import jax, jax.numpy as jnp
from jax import lax
import numpy as np

D_MODEL = 1024
BATCH = 1
SEQ = 256
DEPTH = 4
DEC_BATCH = 1
DEC_SEQ = 32
PAST_LEN = 128

CHUNK = 64
Q_BLOCK = 128
N_MIXERS = 3
N_A = (DEPTH + 2) // 3
N_B = (DEPTH + 1) // 3
N_C = DEPTH // 3
EPS = 1e-6

A_PROJ = 2
A_INNER = A_PROJ * D_MODEL
A_HEADS = 4
A_DH = A_INNER // A_HEADS
A_CONV = 4

B_HEADS = 16
B_DH = D_MODEL // B_HEADS
SB_SCALE = B_DH ** -0.5

C_HEADS = 16
C_Q_RANK = 384
C_KV_RANK = 256
C_NOPE = 64
C_ROPE = 32
C_VDIM = 64
C_SCALE = (C_NOPE + C_ROPE) ** -0.5
ROPE_THETA = 10000.0

D_FF = 4 * D_MODEL

kernel_name = 'hybrid_mlstm_stickbreak_mla_stream_step'

def _rmsnorm(x, g):
    xf = x.astype(jnp.float32)
    y = xf * lax.rsqrt(jnp.mean(xf * xf, axis=-1, keepdims=True) + EPS)
    return (y * g.astype(jnp.float32)).astype(x.dtype)

def _layernorm_heads(h, g):
    mu = jnp.mean(h, axis=-1, keepdims=True)
    var = jnp.mean(jnp.square(h - mu), axis=-1, keepdims=True)
    return (h - mu) * lax.rsqrt(var + EPS) * g

def _rope(x, offset):
    t_len, r = x.shape[1], x.shape[-1]
    half = r // 2
    inv = ROPE_THETA ** (-jnp.arange(half, dtype=jnp.float32) / half)
    ang = (jnp.arange(t_len, dtype=jnp.float32) + offset)[:, None] * inv[None, :]
    ang = ang.reshape((t_len,) + (1,) * (x.ndim - 3) + (half,))
    cos, sin = jnp.cos(ang), jnp.sin(ang)
    xf = x.astype(jnp.float32)
    x1, x2 = xf[..., :half], xf[..., half:]
    return jnp.concatenate([x1 * cos - x2 * sin, x1 * sin + x2 * cos], axis=-1).astype(x.dtype)

def _q_blocks(n_q):
    return [(a, min(a + Q_BLOCK, n_q)) for a in range(0, n_q, Q_BLOCK)]

def _mlstm_chunk(carry, inp):
    C, n, m = carry
    q, k, v, li, lf = inp
    L = q.shape[2]
    b = jnp.cumsum(lf, axis=-1)
    causal = jnp.tril(jnp.ones((L, L), dtype=bool))
    dmat = jnp.where(causal, b[..., :, None] - b[..., None, :] + li[..., None, :], -jnp.inf)
    inter = b + m[..., None]
    m_t = jnp.maximum(inter, jnp.max(dmat, axis=-1))
    w_inter = jnp.exp(inter - m_t)
    s = jnp.einsum('bhtd,bhsd->bhts', q, k) * jnp.exp(dmat - m_t[..., None])
    num = w_inter[..., None] * jnp.einsum('bhtd,bhde->bhte', q, C) + jnp.einsum('bhts,bhse->bhte', s, v)
    nq = w_inter * jnp.einsum('bhtd,bhd->bht', q, n) + jnp.sum(s, axis=-1)
    h = num / jnp.maximum(jnp.abs(nq), jnp.exp(-m_t))[..., None]
    m_new = m_t[..., -1]
    g_state = jnp.exp(b[..., -1] + m - m_new)
    g_tok = jnp.exp(b[..., -1:] - b + li - m_new[..., None])
    C_new = g_state[..., None, None] * C + jnp.einsum('bhs,bhsd,bhse->bhde', g_tok, k, v)
    n_new = g_state[..., None] * n + jnp.einsum('bhs,bhsd->bhd', g_tok, k)
    return (C_new, n_new, m_new), h

def _mlstm_mixer(h, C0, n0, m0, conv0, w_up, conv_w, conv_b, w_q, w_k, w_v, w_gate, b_i, b_f,
                 g_head, skip, w_down):
    f32 = jnp.float32
    bsz, t_len, _ = h.shape
    up = h @ w_up
    xm, z = up[..., :A_INNER], up[..., A_INNER:]
    xpad = jnp.concatenate([conv0.astype(xm.dtype), xm], axis=1)
    xc = conv_b
    for j in range(A_CONV):
        xc = xc + xpad[:, j:j + t_len] * conv_w[j]
    xc = jax.nn.silu(xc)
    xc_h = xc.reshape(bsz, t_len, A_HEADS, A_DH)
    xm_h = xm.reshape(bsz, t_len, A_HEADS, A_DH)
    q = jnp.einsum('bthd,hde->bthe', xc_h, w_q)
    k = jnp.einsum('bthd,hde->bthe', xc_h, w_k) * (A_DH ** -0.5)
    v = jnp.einsum('bthd,hde->bthe', xm_h, w_v)
    gin = jnp.concatenate([q.reshape(bsz, t_len, A_INNER), k.reshape(bsz, t_len, A_INNER),
                           v.reshape(bsz, t_len, A_INNER)], axis=-1)
    g = (gin @ w_gate).astype(f32)
    li = jnp.swapaxes(g[..., :A_HEADS] + b_i, 1, 2)
    lf = jnp.swapaxes(jax.nn.log_sigmoid(g[..., A_HEADS:] + b_f), 1, 2)
    L = CHUNK if t_len % CHUNK == 0 else t_len
    nc = t_len // L

    def to_chunks(a):
        a = a.reshape(a.shape[:2] + (nc, L) + a.shape[3:])
        return jnp.moveaxis(a, 2, 0)

    qh, kh, vh = (jnp.swapaxes(a, 1, 2).astype(f32) for a in (q, k, v))
    carry0 = (C0.astype(f32), n0.astype(f32), m0.astype(f32))
    (C, n, m), hs = lax.scan(_mlstm_chunk, carry0,
                             (to_chunks(qh), to_chunks(kh), to_chunks(vh), to_chunks(li), to_chunks(lf)))
    hs = jnp.moveaxis(hs, 0, 2).reshape(bsz, A_HEADS, t_len, A_DH).transpose(0, 2, 1, 3)
    hn = _layernorm_heads(hs, g_head.reshape(A_HEADS, A_DH).astype(f32)).reshape(bsz, t_len, A_INNER)
    out = (hn.astype(h.dtype) + skip * xc) * jax.nn.sigmoid(z)
    return out @ w_down, (C, n, m, xpad[:, -(A_CONV - 1):])

def _stick_breaking(q, k, v, q_off):
    f32 = jnp.float32
    outs = []
    for a, e in _q_blocks(q.shape[1]):
        nk = max(1, min(k.shape[1], q_off + e - 1))
        qb, kb, vb = q[:, a:e].astype(f32), k[:, :nk].astype(f32), v[:, :nk].astype(f32)
        z = jnp.einsum('bqhd,bkhd->bhqk', qb, kb) * SB_SCALE
        tq = q_off + jnp.arange(a, e)
        before = jnp.arange(nk)[None, :] < tq[:, None]
        log_fail = jnp.where(before, jax.nn.log_sigmoid(-z), 0.0)
        rest = lax.cumsum(log_fail, axis=3, reverse=True) - log_fail
        att = jnp.where(before, jnp.exp(jax.nn.log_sigmoid(z) + rest), 0.0)
        outs.append(jnp.einsum('bhqk,bkhd->bqhd', att, vb))
    return jnp.concatenate(outs, axis=1).astype(q.dtype)

def _sb_mixer(h, k_past, v_past, q_off, w_qkv, w_o):
    bsz, t_len, _ = h.shape
    qkv = (h @ w_qkv).reshape(bsz, t_len, 3, B_HEADS, B_DH)
    q, k, v = qkv[:, :, 0], qkv[:, :, 1], qkv[:, :, 2]
    k_all = k if k_past is None else jnp.concatenate([k_past.astype(k.dtype), k], axis=1)
    v_all = v if v_past is None else jnp.concatenate([v_past.astype(v.dtype), v], axis=1)
    o = _stick_breaking(q, k_all, v_all, q_off)
    return o.reshape(bsz, t_len, D_MODEL) @ w_o, (k, v)

def _mla_attention(q_nope, q_rope, k_nope, v, k_rope, q_off):
    f32 = jnp.float32
    tk = k_nope.shape[1]
    outs = []
    for a, e in _q_blocks(q_nope.shape[1]):
        nk = min(tk, ((q_off + e - 1) // CHUNK + 1) * CHUNK)
        s = (jnp.einsum('bqhd,bkhd->bhqk', q_nope[:, a:e].astype(f32), k_nope[:, :nk].astype(f32))
             + jnp.einsum('bqhr,bkr->bhqk', q_rope[:, a:e].astype(f32), k_rope[:, :nk].astype(f32))) * C_SCALE
        tq = q_off + jnp.arange(a, e)
        vis = (jnp.arange(nk)[None, :] // CHUNK) <= (tq[:, None] // CHUNK)
        p = jax.nn.softmax(jnp.where(vis, s, -jnp.inf), axis=-1)
        outs.append(jnp.einsum('bhqk,bkhd->bqhd', p, v[:, :nk].astype(f32)))
    return jnp.concatenate(outs, axis=1).astype(q_nope.dtype)

def _mla_mixer(h, ckv_past, kr_past, q_off, w_dq, g_q, w_uq, w_dkv, g_kv, w_ukv, w_o):
    bsz, t_len, _ = h.shape
    cq = _rmsnorm(h @ w_dq, g_q)
    q = (cq @ w_uq).reshape(bsz, t_len, C_HEADS, C_NOPE + C_ROPE)
    q_nope, q_rope = q[..., :C_NOPE], _rope(q[..., C_NOPE:], q_off)
    kv_a = h @ w_dkv
    ckv = _rmsnorm(kv_a[..., :C_KV_RANK], g_kv)
    kr = _rope(kv_a[..., C_KV_RANK:], q_off)
    ckv_all = ckv if ckv_past is None else jnp.concatenate([ckv_past.astype(ckv.dtype), ckv], axis=1)
    kr_all = kr if kr_past is None else jnp.concatenate([kr_past.astype(kr.dtype), kr], axis=1)
    kv = jnp.einsum('bsc,chd->bshd', ckv_all, w_ukv)
    o = _mla_attention(q_nope, q_rope, kv[..., :C_NOPE], kv[..., C_NOPE:], kr_all, q_off)
    return o.reshape(bsz, t_len, C_HEADS * C_VDIM) @ w_o, (ckv, kr)

def _sq_relu_mlp(h, w1, w2):
    return jnp.square(jax.nn.relu(h @ w1)) @ w2

def _trunk(x, q_off, st_C, st_n, st_m, st_conv, sb_k, sb_v, mla_ckv, mla_kr,
           norm_mix, norm_mlp, norm_final,
           a_w_up, a_conv_w, a_conv_b, a_w_q, a_w_k, a_w_v, a_w_gate, a_b_i, a_b_f, a_g_head, a_skip, a_w_down,
           b_w_qkv, b_w_o,
           c_w_dq, c_g_q, c_w_uq, c_w_dkv, c_g_kv, c_w_ukv, c_w_o,
           w_ff1, w_ff2):
    new_C, new_n, new_m, new_conv = [], [], [], []
    new_k, new_v, new_ckv, new_kr = [], [], [], []
    for i in range(DEPTH):
        j = i // N_MIXERS
        h = _rmsnorm(x, norm_mix[i])
        if i % N_MIXERS == 0:
            y, (C, n, m, cb) = _mlstm_mixer(h, st_C[j], st_n[j], st_m[j], st_conv[j], a_w_up[j], a_conv_w[j],
                                           a_conv_b[j], a_w_q[j], a_w_k[j], a_w_v[j], a_w_gate[j], a_b_i[j],
                                           a_b_f[j], a_g_head[j], a_skip[j], a_w_down[j])
            new_C.append(C)
            new_n.append(n)
            new_m.append(m)
            new_conv.append(cb)
        elif i % N_MIXERS == 1:
            y, (k, v) = _sb_mixer(h, None if sb_k is None else sb_k[j], None if sb_v is None else sb_v[j],
                                  q_off, b_w_qkv[j], b_w_o[j])
            new_k.append(k)
            new_v.append(v)
        else:
            y, (ckv, kr) = _mla_mixer(h, None if mla_ckv is None else mla_ckv[j],
                                      None if mla_kr is None else mla_kr[j], q_off, c_w_dq[j], c_g_q[j],
                                      c_w_uq[j], c_w_dkv[j], c_g_kv[j], c_w_ukv[j], c_w_o[j])
            new_ckv.append(ckv)
            new_kr.append(kr)
        x = x + y
        x = x + _sq_relu_mlp(_rmsnorm(x, norm_mlp[i]), w_ff1[i], w_ff2[i])
    return (_rmsnorm(x, norm_final), jnp.stack(new_C), jnp.stack(new_n), jnp.stack(new_m), jnp.stack(new_conv),
            jnp.stack(new_k), jnp.stack(new_v), jnp.stack(new_ckv), jnp.stack(new_kr))

def setup_inputs(seed: int = 0) -> dict:
    key = jax.random.key(seed)
    ks = iter(jax.random.split(key, 48))
    f32 = jnp.float32

    def nrm(shape, scale=1.0):
        return jax.random.normal(next(ks), shape, f32) * scale

    def gain(shape):
        return 1.0 + 0.05 * nrm(shape)

    D = D_MODEL
    return {
        'x_prompt': nrm((BATCH, SEQ, D)),
        'x_sample': nrm((DEC_BATCH, DEC_SEQ, D)),
        'state_mlstm_C': nrm((N_A, DEC_BATCH, A_HEADS, A_DH, A_DH), 0.05),
        'state_mlstm_n': nrm((N_A, DEC_BATCH, A_HEADS, A_DH), 0.05),
        'state_mlstm_m': nrm((N_A, DEC_BATCH, A_HEADS)),
        'state_mlstm_conv': nrm((N_A, DEC_BATCH, A_CONV - 1, A_INNER)),
        'cache_sb_k': nrm((N_B, DEC_BATCH, PAST_LEN, B_HEADS, B_DH)),
        'cache_sb_v': nrm((N_B, DEC_BATCH, PAST_LEN, B_HEADS, B_DH)),
        'cache_mla_ckv': nrm((N_C, DEC_BATCH, PAST_LEN, C_KV_RANK)),
        'cache_mla_krope': nrm((N_C, DEC_BATCH, PAST_LEN, C_ROPE)),
        'norm_mix': gain((DEPTH, D)),
        'norm_mlp': gain((DEPTH, D)),
        'norm_final': gain((D,)),
        'a_w_up': nrm((N_A, D, 2 * A_INNER), D ** -0.5),
        'a_conv_w': nrm((N_A, A_CONV, A_INNER), A_CONV ** -0.5),
        'a_conv_b': nrm((N_A, A_INNER), 0.02),
        'a_w_q': nrm((N_A, A_HEADS, A_DH, A_DH), A_DH ** -0.5),
        'a_w_k': nrm((N_A, A_HEADS, A_DH, A_DH), A_DH ** -0.5),
        'a_w_v': nrm((N_A, A_HEADS, A_DH, A_DH), A_DH ** -0.5),
        'a_w_gate': nrm((N_A, 3 * A_INNER, 2 * A_HEADS), (3 * A_INNER) ** -0.5),
        'a_b_i': nrm((N_A, A_HEADS), 0.1),
        'a_b_f': 3.0 + 3.0 * jax.random.uniform(next(ks), (N_A, A_HEADS), f32),
        'a_g_head': gain((N_A, A_INNER)),
        'a_skip': gain((N_A, A_INNER)),
        'a_w_down': nrm((N_A, A_INNER, D), A_INNER ** -0.5),
        'b_w_qkv': nrm((N_B, D, 3 * D), D ** -0.5),
        'b_w_o': nrm((N_B, D, D), D ** -0.5),
        'c_w_dq': nrm((N_C, D, C_Q_RANK), D ** -0.5),
        'c_g_q': gain((N_C, C_Q_RANK)),
        'c_w_uq': nrm((N_C, C_Q_RANK, C_HEADS * (C_NOPE + C_ROPE)), C_Q_RANK ** -0.5),
        'c_w_dkv': nrm((N_C, D, C_KV_RANK + C_ROPE), D ** -0.5),
        'c_g_kv': gain((N_C, C_KV_RANK)),
        'c_w_ukv': nrm((N_C, C_KV_RANK, C_HEADS, C_NOPE + C_VDIM), C_KV_RANK ** -0.5),
        'c_w_o': nrm((N_C, C_HEADS * C_VDIM, D), (C_HEADS * C_VDIM) ** -0.5),
        'w_ff1': nrm((DEPTH, D, D_FF), D ** -0.5),
        'w_ff2': nrm((DEPTH, D_FF, D), D_FF ** -0.5),
    }

def reference(x_prompt, x_sample, state_mlstm_C, state_mlstm_n, state_mlstm_m, state_mlstm_conv,
              cache_sb_k, cache_sb_v, cache_mla_ckv, cache_mla_krope,
              norm_mix, norm_mlp, norm_final,
              a_w_up, a_conv_w, a_conv_b, a_w_q, a_w_k, a_w_v, a_w_gate, a_b_i, a_b_f, a_g_head, a_skip, a_w_down,
              b_w_qkv, b_w_o,
              c_w_dq, c_g_q, c_w_uq, c_w_dkv, c_g_kv, c_w_ukv, c_w_o,
              w_ff1, w_ff2):
    shared = (norm_mix, norm_mlp, norm_final,
              a_w_up, a_conv_w, a_conv_b, a_w_q, a_w_k, a_w_v, a_w_gate, a_b_i, a_b_f, a_g_head, a_skip, a_w_down,
              b_w_qkv, b_w_o,
              c_w_dq, c_g_q, c_w_uq, c_w_dkv, c_g_kv, c_w_ukv, c_w_o,
              w_ff1, w_ff2)
    bp = x_prompt.shape[0]
    z_C = jnp.zeros((N_A, bp, A_HEADS, A_DH, A_DH), jnp.float32)
    z_n = jnp.zeros((N_A, bp, A_HEADS, A_DH), jnp.float32)
    z_m = jnp.zeros((N_A, bp, A_HEADS), jnp.float32)
    z_conv = jnp.zeros((N_A, bp, A_CONV - 1, A_INNER), x_prompt.dtype)
    (y_prompt, p_C, p_n, p_m, p_conv, p_sb_k, p_sb_v, p_ckv, p_krope) = _trunk(
        x_prompt, 0, z_C, z_n, z_m, z_conv, None, None, None, None, *shared)
    past_len = cache_sb_k.shape[2]
    (y_sample, s_C, s_n, s_m, s_conv, s_sb_k, s_sb_v, s_ckv, s_krope) = _trunk(
        x_sample, past_len, state_mlstm_C, state_mlstm_n, state_mlstm_m, state_mlstm_conv,
        cache_sb_k, cache_sb_v, cache_mla_ckv, cache_mla_krope, *shared)
    return (y_prompt, y_sample, p_C, p_n, p_m, p_conv, p_sb_k, p_sb_v, p_ckv, p_krope,
            s_C, s_n, s_m, s_conv, s_sb_k, s_sb_v, s_ckv, s_krope)


_drawn_inputs = setup_inputs


def setup_inputs(seed=0):
    import zlib

    import numpy as np

    out = dict(_drawn_inputs(seed))
    spreads = {}
    factors = {'a_skip': 2.834, 'c_g_q': 8.0}
    for name, (base, spread) in spreads.items():
        noise = np.random.default_rng([zlib.crc32(name.encode()), seed]).standard_normal(out[name].shape)
        drawn = base * np.exp(spread * noise) if base else spread * noise
        out[name] = __import__('jax').numpy.asarray(drawn.astype(out[name].dtype))
    for name, factor in factors.items():
        out[name] = (out[name] * factor).astype(out[name].dtype)
    return out
```

```python
import concourse.bass as bass
from concourse import mybir
from contextlib import ExitStack

F32 = mybir.dt.float32
F32R = mybir.dt.float32r
ACT = mybir.ActivationFunctionType
ALU = mybir.AluOpType
AX_X = mybir.AxisListType.X

D = 1024
TP, TS = 256, 32
T = TP + TS
PAST = 128
DEPTH = 4
EPS = 1e-6
AI, AH, ADH = 2048, 4, 512
BH, BDH = 16, 64
CH, CNOPE, CROPE, CV = 16, 64, 32, 64
CQD = CNOPE + CROPE
CQR, CKR = 384, 256
CSCALE = float(CQD) ** -0.5
DFF = 4096
P = 128
DB = D // P
AB = AI // P
HB_ = ADH // P
TK = T + PAST

RAW = 4
SPL = 4


class Stage:

    def __init__(self, name, tile0, unit0, group0, tiles, units_per_tile, groups):
        self.name = name
        self.n0, self.u0, self.g0 = tile0, unit0, group0
        self.tiles, self.upt, self.groups = tiles, units_per_tile, groups
        self.upg = tiles * units_per_tile // groups
        self.n1, self.u1, self.g1 = tile0 + tiles, unit0 + tiles * units_per_tile, group0 + groups

    def done(self, g):
        return self.u0 + self.upg * (g + 1)


def plan():
    stages, n, u, g = {}, 0, 0, 2
    def add(name, tiles, upt, groups):
        nonlocal n, u, g
        s = stages[name] = Stage(name[0], n, u, g, tiles, upt, groups)
        n, u, g = s.n1, s.u1, s.g1
    for i in range(DEPTH):
        if i % 3 == 0:
            add(("up", i), 32, 2, 8)
            add(("qkv", i), 24, 2, 12)
            add(("down", i), 16, 2, 2)
        elif i % 3 == 1:
            add(("bqkv", i), 24, 2, 6)
            add(("bo", i), 8, 2, 2)
        else:
            add(("dq", i), 4, 2, 1)
            add(("dkv", i), 4, 2, 1)
            add(("uq", i), 8, 3, 8)
            add(("ukv", i), 4, 2, 8)
            add(("co", i), 8, 2, 2)
        add(("ff1", i), 32, 2, 8)
        add(("ff2", i), 32, 2, 2)
    return stages


ST = plan()
TILE_END = {}
for _s in ST.values():
    for _n in range(_s.tiles):
        TILE_END[_s.n0 + _n] = _s.u0 + _s.upt * (_n + 1)

NMIX, NMLP, NFIN, GQ, GKV = 0, 32, 64, 72, 75
CONVW, CONVB, GHEAD, SKIP = 0, 64, 80, 96
CST, N0 = 0, 48


def cols_a(la):
    return 77 + 112 * la


def cols_s(la):
    return 77 + 224 + 64 * la


NCOL = 77 + 224 + 128
SBW = 448
MLW = 416
WIDTH = {"dq": CQR, "dkv": CKR + CROPE}


def hybrid_trunk_kernel(nc, d, o):
    ctx = ExitStack()
    with ctx:
        place = [((nc.sbuf_base + 31) // 32) * 32]

        def at(name, shape, offset, dt=F32):
            return nc.alloc_sbuf_tensor_at(name, shape, dt, offset=offset)

        def take(nbytes):
            off = place[0]
            place[0] += ((nbytes + 31) // 32) * 32
            return off

        BLK = 4 * T
        o_x, o_xg, o_h = take(DB * BLK), take(2 * DB * BLK), take(64 * BLK)
        o_raw, o_hi, o_lo = take(RAW * 4096), take(SPL * 2048), take(SPL * 2048)
        o_mix, o_cp = take(32 * BLK + 24576), take(4096)
        o_tmp = take(4 * 294 * 4)
        X = at("X", [P, DB, T], o_x)
        XGH = at("XGH", [P, DB, T], o_xg, F32R)
        XGL = at("XGL", [P, DB, T], o_xg + DB * BLK, F32R)
        HH = at("HH", [P, 32, T], o_h, F32R)
        HL = at("HL", [P, 32, T], o_h + 32 * BLK, F32R)
        RAWT = at("RAWT", [P, RAW, 1024], o_raw)
        WHI = at("WHI", [P, SPL, 512], o_hi, F32R)
        WLO = at("WLO", [P, SPL, 512], o_lo, F32R)
        TMPX = at("TMPX", [P, 4, 294], o_tmp)
        TMP = at("TMP", [P, 4, T], o_tmp)
        IDENT = at("IDENT", [P, P], take(512))
        ONES = at("ONES", [P, P], take(512))
        COLS = at("COLS", [P, NCOL], take(NCOL * 4))
        RSTD = at("RSTD", [P, T], take(BLK))
        R = at("R", [4, 2 * T + TS], take(4 * (2 * T + TS)))
        ACOL = at("ACOL", [P, 3, 4], take(48))
        CVO = at("CVO", [P, 2, 3, AB], take(2 * 3 * AB * 4))
        NOUT = at("NOUT", [P, 2, AB], take(128))
        SMALL = at("SMALL", [4, 8], take(32))
        assert place[0] <= nc.sbuf_usable_end, (place[0], nc.sbuf_usable_end)
        o_ns = o_mix + 32 * BLK
        SQ = at("SQ", [P, 4, T], o_ns)
        SSUM = at("SSUM", [P, 2, T], o_ns + 4 * BLK)
        NV = at("NV", [P, T], o_ns + 6 * BLK)
        NY = at("NY", [P, T], o_ns + 7 * BLK)
        NT = at("NT", [P, T], o_ns + 8 * BLK)
        XIN = at("XIN", [P, 3, D], o_h)
        VROWS = at("VROWS", [P, 5, P], o_h + 3 * 4 * D)
        SIGZ = at("SIGZ", [P, AB, T], o_mix)
        KT = at("KT", [P, AB, T], o_mix + AB * BLK)
        VTOK = at("VTOK", [P, 3, AI], o_mix + 2 * AB * BLK)
        QT = at("QT", [P, AB, T], o_xg)
        CV_ = at("CV_", [P, 4, 292], o_mix + AB * BLK)
        XCF = at("XCF", [P, 4, T], o_mix + AB * BLK + 4 * 292 * 4)
        CPST = at("CPST", [P, 2, 512], o_cp)
        WG = at("WG", [P, 48, 8], o_cp)
        G8 = at("G8", [8, T], o_cp + 1536)
        CVS = at("CVS", [96, P], o_cp + 1536 + BLK)
        ROWS = at("ROWS", [4, 4, T], o_tmp)
        SX = at("SX", [P, 4, T], o_tmp)
        NST = at("NST", [32, P], o_tmp)
        VT_ = at("VT_", [P, AB, T], o_h + 16 * BLK)
        oa = o_h + 16 * BLK
        KG = at("KG", [P, 3, 512], oa)
        DT = at("DT", [P, MLW], oa + 6144)
        PT_ = at("PT_", [P, MLW], oa + 6144 + 4 * MLW)
        EM = at("EM", [P, T], oa + 6144 + 8 * MLW)
        WB = at("WB", [P, 2, TS], oa + 6144 + 8 * MLW + BLK)
        QW = at("QW", [P, 2, 4, TS], oa + 6144 + 8 * MLW + BLK + 256)
        HB = at("HB", [P, 4, T], oa + 6144 + 8 * MLW + BLK + 256 + 1024)
        MASKM = at("MASKM", [P, MLW], oa + 6144 + 8 * MLW + BLK + 256 + 1024 + 4 * BLK)
        assert 6144 + 12 * MLW + BLK + 256 + 1024 + 4 * BLK <= 16 * BLK
        ob = o_h + 48 * BLK
        C0 = at("C0", [P, 2, 4, 512], ob)
        SEL = at("SEL", [4, 4, P], ob + 16384)
        BQ = at("BQ", [P, DB, T], o_mix)
        BK = at("BK", [P, DB, 384], o_mix + DB * BLK)
        BKP = at("BKP", [P, DB, PAST], o_mix + DB * BLK + 12288)
        BATT = at("BATT", [P, 3, SBW], o_mix + DB * BLK + 12288 + 4096)
        BMASK = at("BMASK", [P, SBW], o_mix + DB * BLK + 12288 + 4096 + 12 * SBW)
        BTRI = at("BTRI", [P, 2, P], o_mix + DB * BLK + 12288 + 4096 + 16 * SBW)
        assert DB * BLK + 12288 + 4096 + 16 * SBW + 1024 <= 32 * BLK
        oa = o_h + 8 * BLK
        BV = at("BV", [P, DB, T], oa)
        BVT = at("BVT", [P, 3, D], oa + DB * BLK)
        BVP = at("BVP", [P, D], oa + DB * BLK + 12288)
        ob = o_h + 40 * BLK
        BKT = at("BKT", [P, 3, D], ob)
        BKPT = at("BKPT", [P, D], ob + 12288)
        BE = at("BE", [P, 3, SBW], ob + 16384)
        BSP = at("BSP", [P, 3, SBW], ob + 16384 + 12 * SBW)
        CQ96 = at("CQ96", [CQD, CH, T], o_mix)
        CK96 = at("CK96", [CQD, CH, TK], o_mix + CH * BLK)
        CVT = at("CVT", [P, 4, 1024], o_mix + CH * BLK + CH * TK * 4)
        CKRO = at("CKRO", [32, TK], o_cp)
        CKR_ = at("CKR_", [32, T], o_cp + 4 * TK)
        KRT = at("KRT", [32, T], o_tmp)
        oa = o_h + 8 * BLK
        CQF = at("CQF", [P, 3, T], oa)
        CKF = at("CKF", [P, 2, T], oa + 3 * BLK)
        CKV = at("CKV", [P, 2, TK], oa + 5 * BLK)
        CSQ = at("CSQ", [P, 3, T], oa + 5 * BLK + 8 * TK)
        CV3 = at("CV3", [P, 3, 2, T], oa + 8 * BLK + 8 * TK)
        CRST = at("CRST", [P, 2, T], oa + 14 * BLK + 8 * TK)
        KROPE = at("KROPE", [32, 2, T], o_mix + 42 * BLK)
        KPERM = at("KPERM", [32, 32], o_mix + 44 * BLK)
        CPAST = at("CPAST", [P, 288], oa + 16 * BLK + 8 * TK)
        COUT = at("COUT", [P, 3, 288], oa + 17 * BLK + 8 * TK)
        assert 20 * BLK + 8 * TK <= 24 * BLK
        CSS = at("CSS", [P, 2, T], o_tmp + 2 * BLK)
        ob = o_h + 40 * BLK
        CQH = at("CQH", [P, 3, T], ob, F32R)
        CQL = at("CQL", [P, 3, T], ob + 3 * BLK, F32R)
        CKH = at("CKH", [P, 2, TK], ob + 6 * BLK, F32R)
        CKL = at("CKL", [P, 2, TK], ob + 6 * BLK + 8 * TK, F32R)
        ob += 6 * BLK + 16 * TK
        COSS = at("COSS", [CQD, 2, T], ob)
        PERM = at("PERM", [CQD, CQD], ob + 2 * BLK)
        BMROW = at("BMROW", [1, 192], ob + 2 * BLK + 384)
        ob += 2 * BLK + 384 + 768
        PB = at("PB", [P, 2, 384], ob)
        PTB = at("PTB", [P, 2, 384], ob + 3072)
        CPS = at("CPS", [P, 160], ob + 6144)
        CPTS = at("CPTS", [P, 2, 2, P], ob + 6144 + 640)
        CST_ = at("CST_", [P, 2, 4, 2], ob + 6144 + 640 + 2048)
        CSTS = at("CSTS", [P, 4], ob + 6144 + 640 + 2048 + 64)
        assert ob + 6144 + 640 + 2048 + 96 <= o_h + 64 * BLK
        YF = at("YF", [P, DB, T], o_xg)
        YO = at("YO", [P, 3, D], o_h)

        PS = ctx.enter_context(nc.psum_tensor("PS", [P, 8, 512], F32))

        def sem(name):
            return ctx.enter_context(nc.semaphore(name))

        weight_in = [sem(f"weight_in{i}") for i in range(RAW)]
        weight_hi = sem("weight_hi_ready")
        weight_lo = sem("weight_lo_ready")
        unit_done = sem("unit_done")
        group_out = sem("group_out")
        ukv_done = sem("ukv_done")
        dve_own = sem("dve_own")
        act_own = sem("act_own")
        pool_own = sem("pool_own")
        const_in, rows_in, x_in = sem("const_in"), sem("rows_in"), sem("x_in")
        xpose_done, cols_out = sem("xpose_done"), sem("cols_out")
        xg_hi, xg_lo, ssum = sem("xg_hi"), sem("xg_lo"), sem("ssum")
        stat_done, var_out, y_out = sem("stat_done"), sem("var_out"), sem("y_out")
        h_sq, h_hi, h_lo = sem("h_sq"), sem("h_hi"), sem("h_lo")
        conv_first, conv_done, xc_out, xc_hi, xc_lo, xm_hi, xm_lo, sigz_out = [
            sem(n) for n in ("conv_first", "conv_done", "xc_out", "xc_hi", "xc_lo", "xm_hi", "xm_lo", "sigz_out")]
        mconst_in, gates_done, g8_out, gsel_done, f_out, fabs_out, rows_out = [
            sem(n) for n in ("mconst_in", "gates_done", "g8_out", "gsel_done", "f_out", "fabs_out", "rows_out")]
        mask_in, sel_in = sem("mask_in"), sem("sel_in")
        acol_done, vxp_done, vxp_out = [sem(n) for n in ("acol_done", "vxp_done", "vxp_out")]
        bcast_done, score_done, darg_out, dexp_out, em_out, dmask_out, prob_out, qw_out = [
            sem(n) for n in ("bcast_done", "score_done", "darg_out", "dexp_out", "em_out", "dmask_out",
                             "prob_out", "qw_out")]
        kxp_done, kg_out, num_done, hnum_out, mean_done, hc_out, hsq_out, hvar_done = [
            sem(n) for n in ("kxp_done", "kg_out", "num_done", "hnum_out", "mean_done", "hc_out", "hsq_out",
                             "hvar_done")]
        cp_done, cp_out, cs_done, cs_out, n_done, n_out = [
            sem(n) for n in ("cp_done", "cp_out", "cs_done", "cs_out", "n_done", "n_out")]
        hv_out, hy_out, sx_out, mo_out, mh_hi, mh_lo = [
            sem(n) for n in ("hv_out", "hy_out", "sx_out", "mo_out", "mh_hi", "mh_lo")]
        c0_in = [sem(f"c0_in{i}") for i in range(2)]
        cp_dma = [sem(f"cp_dma{i}") for i in range(2)]
        cs_dma = [sem(f"cs_dma{i}") for i in range(2)]
        cvs_done, cvs_out, cvs_dma, nst_done, nst_out, nst_dma, m_out, m_dma = [
            sem(n) for n in ("cvs_done", "cvs_out", "cvs_dma", "nst_done", "nst_out", "nst_dma", "m_out", "m_dma")]
        b_in, bxp_done, bxp_out, b_dma, bpad = [sem(n) for n in ("b_in", "bxp_done", "bxp_out", "b_dma", "bpad")]
        babs_out = sem("babs_out")
        bz_done, be_out, bsp_out, bspm_out, bs_done, bt_out, batt_out, battm_out, bo_done, bo_hi, bo_lo = [
            sem(n) for n in ("bz_done", "be_out", "bsp_out", "bspm_out", "bs_done", "bt_out", "batt_out",
                             "battm_out", "bo_done", "bo_hi", "bo_lo")]
        c_in, css_out, cstat_done, cv_out, cy_out, cq_hi, cq_lo, ckv_out, ck_hi, ck_lo, kro_out, crep_out = [
            sem(n) for n in ("c_in", "css_out", "cstat_done", "cv_out", "cy_out", "cq_hi", "cq_lo", "ckv_out",
                             "ck_hi", "ck_lo", "kro_out", "crep_out")]
        cxp_done, cxp_out, c_dma, rot_done, rot_out = [
            sem(n) for n in ("cxp_done", "cxp_out", "c_dma", "rot_done", "rot_out")]
        cs_sc, c_max, c_exp, c_nrm, c_xp, c_pt, c_o, c_ohi, c_olo = [
            sem(n) for n in ("c_scores_done", "c_max_out", "c_exp_out", "c_norm_out", "c_xpose_done", "c_pt_out",
                             "c_o_done", "c_o_hi", "c_o_lo")]
        ss_sc, ss_max, ss_exp, ss_nrm, ss_xp, ss_pt = [
            sem(n) for n in ("s_scores_done", "s_max_out", "s_exp_out", "s_norm_out", "s_xpose_done", "s_pt_out")]
        yf_out, yo_done, yo_out, y_dma = [sem(n) for n in ("yf_out", "yo_done", "yo_out", "y_dma")]

        block = ctx.enter_context(nc.Block())

        TBS = [(0, 0, P), (1, P, P), (2, TP, TS)]

        def gain(nu):
            i, mlp = divmod(nu, 2)
            return NFIN if nu == 2 * DEPTH else (NMLP if mlp else NMIX) + DB * i

        @block.sync
        def _(sp):
            def dma(out, in_, s):
                sp.dma_start(out, in_).then_inc(s, 16)

            def slot_free(n):
                if n >= RAW:
                    sp.wait_ge(weight_lo, TILE_END[n - RAW])

            def tile(st, t, src):
                n, (k, m) = st.n0 + t, (src.shape[0] // P, src.shape[1])
                slot_free(n)
                dst = RAWT[:, n % RAW, 0:k * m].rearrange("p (k m) -> p k m", k=k)
                dma(dst, src.rearrange("(k p) m -> p k m", p=P), weight_in[n % RAW])

            def looped(st, w, g0, g1):
                with sp.Fori(g0, g1) as g:
                    for c in range(4):
                        sp.wait_ge(weight_lo, 8 * g + (st.u0 + 2 * c - 6))
                        dma(RAWT[:, c, :].rearrange("p (k m) -> p k m", k=2),
                            w[2 * c * P:2 * (c + 1) * P, bass.ds(g * 512, 512)].rearrange("(k p) m -> p k m", p=P),
                            weight_in[c])

            def group_tiles(st, w, first):
                for c in range(4):
                    tile(st, c, w[2 * c * P:2 * (c + 1) * P, 0:512])

            dma(IDENT[:], d["const_pp"][0], const_in)
            dma(ONES[:], d["const_pp"][1], const_in)
            dma(XIN[:, 0:2, :], d["x_prompt"][0].rearrange("(a p) f -> p a f", p=P), x_in)
            dma(XIN[0:TS, 2, :], d["x_sample"][0], x_in)

            def rows(row, slot, src):
                n = src.shape[0]
                dma(VROWS[row:row + n, slot, :], src, rows_in)

            rows(NMIX, 0, d["norm_mix"].rearrange("i (b f) -> (i b) f", f=P))
            rows(NMLP, 0, d["norm_mlp"].rearrange("i (b f) -> (i b) f", f=P))
            rows(NFIN, 0, d["norm_final"].rearrange("(b f) -> b f", f=P))
            rows(GQ, 0, d["c_g_q"].rearrange("i (b f) -> (i b) f", f=P))
            rows(GKV, 0, d["c_g_kv"].rearrange("i (b f) -> (i b) f", f=P))
            for la in range(2):
                rows(CONVW, 1 + la, d["a_conv_w"][la].rearrange("j (b f) -> (j b) f", f=P))
                rows(CONVB, 1 + la, d["a_conv_b"][la].rearrange("(b f) -> b f", f=P))
                rows(GHEAD, 1 + la, d["a_g_head"][la].rearrange("(b f) -> b f", f=P))
                rows(SKIP, 1 + la, d["a_skip"][la].rearrange("(b f) -> b f", f=P))
                rows(CST, 3 + la, d["state_mlstm_conv"][la, 0].rearrange("j (b f) -> (j b) f", f=P))
                rows(N0, 3 + la, d["state_mlstm_n"][la, 0].rearrange("h (b f) -> (h b) f", f=P))
                for c, name in enumerate(("a_b_i", "a_b_f")):
                    dma(SMALL[:, 2 * c + la:2 * c + la + 1], d[name][la].rearrange("(h a) -> h a", a=1), rows_in)
                dma(SMALL[:, 4 + la:5 + la], d["state_mlstm_m"][la, 0].rearrange("(h a) -> h a", a=1), rows_in)

            for i in range(DEPTH):
                if i % 3 == 0:
                    la = i // 3
                    st, w = ST["up", i], d["a_w_up"][la]
                    group_tiles(st, w, True)
                    looped(st, w, 1, 8)
                    if la:
                        for b in range(2):
                            sp.wait_ge(cp_dma[b], 16 * 8 * la)
                        sp.wait_ge(cvs_dma, 32 * la)
                    dma(WG[:], d["a_w_gate"][la].rearrange("(k p) g -> p k g", p=P), mconst_in)
                    st = ST["qkv", i]
                    for h in range(AH):
                        for m, name in enumerate(("a_w_q", "a_w_k", "a_w_v")):
                            for t in range(2):
                                tile(st, 6 * h + 2 * m + t, d[name][la, h, 2 * t * P:2 * (t + 1) * P, :])
                    down, w = ST["down", i], d["a_w_down"][la]

                    def down_tile(t):
                        g, c = divmod(t, 8)
                        tile(down, t, w[2 * c * P:2 * (c + 1) * P, 512 * g:512 * (g + 1)])

                    for t in range(4):
                        down_tile(t)
                    sp.wait_ge(unit_done, st.u1)
                    dma(SEL[:], d["const_sel"], sel_in)
                    for h in range(2):
                        dma(C0[:, h], d["state_mlstm_C"][la, 0, h].rearrange("(b p) e -> p b e", p=P), c0_in[h])
                    sp.wait_ge(cvs_out, la + 1)
                    dma(o["p_conv"][la, 0].rearrange("j (b f) -> (j b) f", f=P), CVS[0:48, :], cvs_dma)
                    dma(o["s_conv"][la, 0].rearrange("j (b f) -> (j b) f", f=P), CVS[48:96, :], cvs_dma)
                    sp.wait_ge(vxp_out, 12 * (la + 1))
                    dma(MASKM[:], d["const_mask_ml"], mask_in)
                    sp.wait_ge(m_out, la + 1)
                    dma(o["p_m"][la, 0].rearrange("(h a) -> h a", a=1), SMALL[:, 6:7], m_dma)
                    dma(o["s_m"][la, 0].rearrange("(h a) -> h a", a=1), SMALL[:, 7:8], m_dma)
                    for h in range(AH):
                        U = AH * la + h
                        for b in range(4):
                            q = 4 * U + b
                            sp.wait_ge(cp_out, q + 1)
                            dma(o["p_C"][la, 0, h, b * P:(b + 1) * P, :], CPST[:, q % 2], cp_dma[q % 2])
                        sp.wait_ge(cs_out, U + 1)
                        dma(o["s_C"][la, 0, h].rearrange("(b p) e -> p b e", p=P), C0[:, h % 2], cs_dma[h % 2])
                        if h + 2 < AH:
                            sp.wait_ge(cs_dma[h % 2], 16 * (2 * la + h // 2 + 1))
                            dma(C0[:, h % 2], d["state_mlstm_C"][la, 0, h + 2].rearrange("(b p) e -> p b e", p=P),
                                c0_in[h % 2])
                    sp.wait_ge(nst_out, la + 1)
                    dma(o["p_n"][la, 0].rearrange("h (b f) -> (h b) f", f=P), NST[0:16, :], nst_dma)
                    dma(o["s_n"][la, 0].rearrange("h (b f) -> (h b) f", f=P), NST[16:32, :], nst_dma)
                    for t in range(4, 16):
                        down_tile(t)
                elif i % 3 == 1:
                    st, w = ST["bqkv", i], d["b_w_qkv"][0]
                    group_tiles(st, w, True)
                    dma(BMASK[:], d["const_mask_sb"], b_in)
                    dma(BTRI[:, 0], d["const_pp"][2], b_in)
                    dma(BTRI[:, 1], d["const_pp"][3], b_in)
                    looped(st, w, 1, 6)
                    dma(BKPT[:], d["cache_sb_k"][0, 0].rearrange("s h f -> s (h f)"), b_in)
                    dma(BVP[:], d["cache_sb_v"][0, 0].rearrange("s h f -> s (h f)"), b_in)
                    st, w = ST["bo", i], d["b_w_o"][0]
                    for t in range(4):
                        tile(st, t, w[2 * t * P:2 * (t + 1) * P, 0:512])
                    sp.wait_ge(bxp_out, 14)
                    for tok, name in ((BKT, "k"), (BVT, "v")):
                        dma(o[f"p_sb_{name}"][0, 0].rearrange("(a p) h f -> p a (h f)", p=P), tok[:, 0:2], b_dma)
                        dma(o[f"s_sb_{name}"][0, 0].rearrange("p h f -> p (h f)"), tok[0:TS, 2], b_dma)
                    for t in range(4, 8):
                        g, c = divmod(t, 4)
                        tile(st, t, w[2 * c * P:2 * (c + 1) * P, 512 * g:512 * (g + 1)])
                else:
                    st, w = ST["dq", i], d["c_w_dq"][0]
                    for t in range(4):
                        tile(st, t, w[2 * t * P:2 * (t + 1) * P, :])
                    st, w = ST["dkv", i], d["c_w_dkv"][0]
                    for t in range(4):
                        tile(st, t, w[2 * t * P:2 * (t + 1) * P, :])
                    dma(CPAST[:, 0:CKR], d["cache_mla_ckv"][0, 0], c_in)
                    dma(CPAST[:, CKR:CKR + CROPE], d["cache_mla_krope"][0, 0], c_in)
                    dma(COSS[:], d["const_rope"], c_in)
                    dma(PERM[:], d["const_perm"], c_in)
                    dma(BMROW[:], d["const_bmrow"], c_in)
                    dma(KROPE[:], d["const_rope_k"], c_in)
                    dma(KPERM[:], d["const_perm_k"], c_in)
                    st, w = ST["uq", i], d["c_w_uq"][0]
                    for t in range(8):
                        tile(st, t, w[:, 2 * CQD * t:2 * CQD * (t + 1)])
                    st, w = ST["ukv", i], d["c_w_ukv"][0].rearrange("c h e -> c (h e)")
                    for t in range(4):
                        tile(st, t, w[:, 512 * t:512 * (t + 1)])
                    sp.wait_ge(cxp_out, 3)
                    dma(o["p_ckv"][0, 0].rearrange("(a p) f -> p a f", p=P), COUT[:, 0:2, 0:CKR], c_dma)
                    dma(o["p_krope"][0, 0].rearrange("(a p) f -> p a f", p=P), COUT[:, 0:2, CKR:CKR + CROPE], c_dma)
                    dma(o["s_ckv"][0, 0], COUT[0:TS, 2, 0:CKR], c_dma)
                    dma(o["s_krope"][0, 0], COUT[0:TS, 2, CKR:CKR + CROPE], c_dma)
                    st, w = ST["co", i], d["c_w_o"][0]
                    for t in range(8):
                        g, c = divmod(t, 4)
                        tile(st, t, w[2 * c * P:2 * (c + 1) * P, 512 * g:512 * (g + 1)])
                st, w = ST["ff1", i], d["w_ff1"][i]
                group_tiles(st, w, True)
                looped(st, w, 1, 8)
                st, w = ST["ff2", i], d["w_ff2"][i]
                for g in range(2):
                    for c in range(4):
                        tile(st, 16 * g + c, w[2 * c * P:2 * (c + 1) * P, 512 * g:512 * (g + 1)])
                    with sp.Fori(1, 4) as j:
                        for c in range(4):
                            sp.wait_ge(weight_lo, 8 * j + (st.u0 + 32 * g + 2 * c - 6))
                            dma(RAWT[:, c, :].rearrange("p (k m) -> p k m", k=2),
                                w[bass.ds(j * 1024 + c * 256, 256), 512 * g:512 * (g + 1)].rearrange(
                                    "(k p) m -> p k m", p=P), weight_in[c])
            sp.wait_ge(yo_out, 6)
            dma(o["y_prompt"][0].rearrange("(a p) f -> p a f", p=P), YO[:, 0:2], y_dma)
            dma(o["y_sample"][0], YO[0:TS, 2], y_dma)
            for s, n in ((y_dma, 32), (b_dma, 64), (c_dma, 64), (cvs_dma, 64), (nst_dma, 64), (m_dma, 64),
                         (cp_dma[0], 256), (cp_dma[1], 256), (cs_dma[0], 64), (cs_dma[1], 64)):
                sp.wait_ge(s, n)

        def stream(e, st, split, first=None, late_first=None, after=None, late=None, loop=False, at=5):
            n = st.upg
            at_late = min(at, n - 1)
            at_hook = min(3, n - 1) if e is nc.scalar else 2

            def group(g, b, chunk0, prev):
                for i in range(min(n, 8)):
                    split(st, chunk0 if n >= 8 else None, i if n >= 8 else n * g + i)
                    if i == at_hook:
                        if prev is None:
                            first and first()
                        else:
                            after and after(prev, b ^ 1)
                    if i == at_late:
                        if prev is None:
                            late_first and late_first()
                        else:
                            late and late(prev)
                if n > 8:
                    with e.Fori(1, n // 8) as j:
                        for i in range(8):
                            split(st, chunk0 + j, i)

            if n == 8 and loop:
                group(0, 0, 0, None)
                group(1, 1, 1, 0)
                with e.Fori(1, st.groups // 2) as q:
                    group(2 * q, 0, 2 * q, 2 * q - 1)
                    group(2 * q + 1, 1, 2 * q + 1, 2 * q)
            else:
                for g in range(st.groups):
                    group(g, g % 2, g * n // 8, g - 1 if g else None)

        @block.scalar
        def _(act):
            own = [0]

            def link(ins):
                own[0] += 1
                ins.then_inc(act_own, 1)
                act.wait_ge(act_own, own[0])

            def split(st, j, c):
                if st.upt == 2:
                    if j is None:
                        j, c = divmod(c, 8)
                    slot, kk = c // 2, c % 2
                    if kk == 0:
                        act.wait_ge(weight_in[slot], 16 * j + (16 * (st.n0 // 4) + 16))
                    u = st.u0 + 8 * j + c
                    if not isinstance(u, int) or u >= SPL:
                        act.wait_ge(unit_done, 8 * j + (st.u0 + c - SPL + 1))
                    w = WIDTH.get(st.name, 512)
                    act.activation(WHI[:, c % SPL, 0:w], RAWT[:, slot, kk * w:(kk + 1) * w], ACT.Copy) \
                       .then_inc(weight_hi, 1)
                else:
                    t, k = divmod(c, 3)
                    if k == 0:
                        act.wait_ge(weight_in[t % RAW], 16 * ((st.n0 + t) // RAW + 1))
                    act.wait_ge(unit_done, st.u0 + c - SPL + 1)
                    act.activation(WHI[:, (st.u0 + c) % SPL, 0:192], RAWT[:, t % RAW, 192 * k:192 * (k + 1)],
                                   ACT.Copy).then_inc(weight_hi, 1)

            def norm_hi(nu, half, g):
                act.wait_ge(group_out, g + 1)
                for b in range(4):
                    f = 4 * half + b
                    ins = act.activation(XGH[:, f, :], X[:, f, :], ACT.Copy,
                                         scale=COLS[:, gain(nu) + f:gain(nu) + f + 1])
                ins.then_inc(xg_hi, 1)

            def norm_y(nu):
                act.wait_ge(var_out, nu + 1)
                link(act.activation(NY[:], NV[:], ACT.Ln))
                act.activation(NY[:], NY[:], ACT.Exp, scale=-0.5).then_inc(y_out, 1)

            norm_hi(0, 0, 0)
            last = [lambda: norm_hi(0, 1, 1), None]

            def mlstm_up(i, la):
                st = ST["up", i]

                def after(g, b):
                    k = 4 * la + g
                    if g == 0:
                        norm_y(2 * i)
                    act.wait_ge(group_out, st.g0 + g + 1)
                    if g < 4:
                        for a in range(4):
                            f = 4 * g + a
                            w0 = cols_a(la) + CONVW + f
                            b0 = cols_a(la) + CONVB + f
                            ins = act.activation(CV_[:, a, 0:291], TMPX[:, a, 0:291], ACT.Identity,
                                                 bias=COLS[:, b0:b0 + 1], scale=COLS[:, w0:w0 + 1])
                        ins.then_inc(conv_first, 1)
                        act.activation(HH[:, 16 + 4 * g:20 + 4 * g, 0:TP], TMPX[:, :, 3:3 + TP], ACT.Copy)
                        act.activation(HH[:, 16 + 4 * g:20 + 4 * g, TP:T], TMPX[:, :, 262:294], ACT.Copy) \
                           .then_inc(xm_hi, 1)
                    else:
                        z = 4 * (g - 4)
                        act.activation(SIGZ[:, z:z + 4, :], TMP[:], ACT.Sigmoid).then_inc(sigz_out, 1)

                def late(g):
                    if g < 4:
                        k = 4 * la + g
                        act.wait_ge(conv_done, k + 1)
                        if k:
                            act.wait_ge(xc_lo, k)
                        act.activation(XCF[:, :, 0:TP], CV_[:, :, 0:TP], ACT.Silu)
                        act.activation(XCF[:, :, TP:T], CV_[:, :, 259:291], ACT.Silu).then_inc(xc_out, 1)
                        act.wait_ge(xc_out, k + 1)
                        act.activation(HH[:, 4 * g:4 * g + 4, :], XCF[:], ACT.Copy).then_inc(xc_hi, 1)

                stream(act, st, split, last[0], last[1], after, late, at=7)
                last[:] = [lambda: after(7, 1), None]

            def mlstm_mix(i, la):
                act.wait_ge(cvs_done, la + 1)
                act.activation(CVS[:], PS[0:96, 3, 0:P], ACT.Copy).then_inc(cvs_out, 1)

                def vtok(x):
                    h, tb = divmod(x, 3)
                    n = TBS[tb][2]
                    act.wait_ge(vxp_done, 12 * la + x + 1)
                    act.activation(VTOK[0:n, tb, 512 * h:512 * (h + 1)], PS[0:n, 4 + x % 4, :], ACT.Copy) \
                       .then_inc(vxp_out, 1)

                for x in range(3):
                    vtok(x)
                act.wait_ge(f_out, la + 1)
                link(act.activation(ROWS[:, 1, :], ROWS[:, 1, :], ACT.Exp))
                act.activation(ROWS[:, 1, :], ROWS[:, 1, :], ACT.Ln, bias=1.0).then_inc(fabs_out, 1)
                for x in range(3, 12):
                    vtok(x)

                def decay(h):
                    U = AH * la + h
                    act.wait_ge(darg_out, U + 1)
                    act.activation(DT[:, 0:384], DT[:, 0:384], ACT.Exp)
                    act.activation(DT[0:TS, 384:416], DT[0:TS, 384:416], ACT.Exp).then_inc(dexp_out, 1)
                    act.activation(EM[:], PS[:, 1, 0:T], ACT.Exp)
                    act.activation(WB[:, h % 2, :], PS[:, 1, T:T + TS], ACT.Exp).then_inc(em_out, 1)

                decay(0)
                act.wait_ge(cvs_dma, 32 * (la + 1))
                for h in range(AH):
                    U = AH * la + h
                    if h + 1 < AH:
                        decay(h + 1)
                    for b in range(4):
                        q = 4 * U + b
                        act.wait_ge(cp_done, q + 1)
                        if q >= 2:
                            act.wait_ge(cp_dma[q % 2], 16 * (q // 2))
                        act.activation(CPST[:, q % 2, :], PS[:, 4 + b, :], ACT.Copy).then_inc(cp_out, 1)
                    act.wait_ge(hc_out, U + 1)
                    act.activation(QT[:, 4 * h:4 * h + 4, :], HB[:], ACT.Square).then_inc(hsq_out, 1)
                    act.wait_ge(hv_out, U + 1)
                    link(act.activation(KT[:, 4 * h + 1, :], KT[:, 4 * h, :], ACT.Ln))
                    act.activation(KT[:, 4 * h + 1, :], KT[:, 4 * h + 1, :], ACT.Exp, scale=-0.5).then_inc(hy_out, 1)
                    act.wait_ge(mo_out, U + 1)
                    act.activation(HH[:, 4 * h:4 * h + 4, :], HB[:], ACT.Copy).then_inc(mh_hi, 1)
                act.wait_ge(nst_done, la + 1)
                act.activation(NST[:], PS[0:32, 0, 0:P], ACT.Copy).then_inc(nst_out, 1)

            def sb_mix(i):
                for x in range(14):
                    act.wait_ge(bxp_done, x + 1)
                    if x < 2:
                        act.activation(BKP[:, 4 * x:4 * x + 4, :], PS[:, x % 8, :].rearrange("p (b t) -> p b t", b=4),
                                       ACT.Copy).then_inc(bxp_out, 1)
                    else:
                        kv, y = divmod(x - 2, 6)
                        tb, half = divmod(y, 2)
                        n = TBS[tb][2]
                        act.activation((BVT, BKT)[kv][0:n, tb, 512 * half:512 * (half + 1)], PS[0:n, x % 8, :],
                                       ACT.Copy).then_inc(bxp_out, 1)
                for s in range(BH + 4):
                    h = s
                    if h < BH:
                        act.wait_ge(babs_out, h + 1)
                        link(act.activation(BE[:, h % 3, :], BE[:, h % 3, :], ACT.Exp))
                        act.activation(BE[:, h % 3, :], BE[:, h % 3, :], ACT.Ln, bias=1.0).then_inc(be_out, 1)
                    h = s - 2
                    if 0 <= h < BH:
                        act.wait_ge(bt_out, h + 1)
                        act.activation(BATT[:, h % 3, :], BATT[:, h % 3, :], ACT.Exp).then_inc(batt_out, 1)
                    h = s - 4
                    if h >= 0 and h % 2:
                        act.wait_ge(bo_done, h + 1)
                        act.activation(HH[:, h // 2, :], PS[:, 5 + h // 2 % 2, 0:T], ACT.Copy).then_inc(bo_hi, 1)

            def mla_prep(i):
                act.wait_ge(cv_out, 1)
                link(act.activation(CV3[:, 1], CV3[:, 0], ACT.Ln))
                act.activation(CV3[:, 1], CV3[:, 1], ACT.Exp, scale=-0.5).then_inc(cy_out, 1)
                for b in range(3):
                    ins = act.activation(CQH[:, b, :], CQF[:, b, :], ACT.Copy, scale=COLS[:, GQ + b:GQ + b + 1])
                ins.then_inc(cq_hi, 1)
                act.wait_ge(ckv_out, 1)
                act.activation(CKH[:], CKV[:], ACT.Copy).then_inc(ck_hi, 1)
                act.wait_ge(kro_out, 1)
                for q in range(4):
                    ins = act.activation(CK96[64:96, 4 * q:4 * q + 4, :],
                                         CKRO[:, :].unsqueeze(1).to_broadcast([32, 4, TK]), ACT.Copy)
                ins.then_inc(crep_out, 1)
                for tb, _, n in TBS:
                    act.wait_ge(cxp_done, tb + 1)
                    act.activation(COUT[0:n, tb, :], PS[0:n, 4 + tb, 0:288], ACT.Copy).then_inc(cxp_out, 1)

            def mla_mix(i):
                for s in range(CH + 3):
                    h = s
                    if h < CH and h % 4 == 0:
                        g = h // 4
                        act.wait_ge(ss_max, g + 1)
                        act.activation(CPS[:], PS[:, 6, 0:160], ACT.Exp, bias=CSTS[:, 1:2], scale=CSCALE,
                                       accum_out=CSTS[:, 2:3]).then_inc(ss_exp, 1)
                        act.wait_ge(ss_xp, g + 1)
                        act.activation(CPTS[:, g % 2, 0, :], PS[:, 7, 0:P], ACT.Copy)
                        act.activation(CPTS[0:TS, g % 2, 1, :], PS[0:TS, 7, P:2 * P], ACT.Copy).then_inc(ss_pt, 1)
                    if h < CH:
                        act.wait_ge(c_max, h + 1)
                        if h >= 2:
                            act.wait_ge(c_xp, h - 1)
                        act.activation(PB[:, h % 2, 0:128], PS[:, h % 2, 0:128], ACT.Exp,
                                       bias=CST_[:, h % 2, 1, 0:1], scale=CSCALE, accum_out=CST_[:, h % 2, 2, 0:1])
                        act.activation(PB[:, h % 2, 128:384], PS[:, h % 2, 128:384], ACT.Exp,
                                       bias=CST_[:, h % 2, 1, 1:2], scale=CSCALE,
                                       accum_out=CST_[:, h % 2, 2, 1:2]).then_inc(c_exp, 1)
                    h = s - 2
                    if 0 <= h < CH:
                        act.wait_ge(c_xp, h + 1)
                        act.activation(PTB[:, h % 2, :], PS[:, 2 + h % 2, 0:384], ACT.Copy).then_inc(c_pt, 1)
                    h = s - 3
                    if h >= 0 and h % 2:
                        act.wait_ge(c_o, h + 1)
                        act.activation(HH[:, h // 2, :], PS[:, 4 + h // 2 % 2, 0:T], ACT.Copy).then_inc(c_ohi, 1)

            for i in range(DEPTH):
                la = i // 3
                if i % 3 == 0:
                    mlstm_up(i, la)
                    stream(act, ST["qkv", i], split, last[0])
                    stream(act, ST["down", i], split, lambda: mlstm_mix(i, la), None,
                           lambda g, b: norm_hi(2 * i + 1, g, ST["down", i].g0 + g))
                    res = ST["down", i]
                elif i % 3 == 1:
                    stream(act, ST["bqkv", i], split, last[0], last[1], lambda g, b: norm_y(2 * i) if g == 0 else None)
                    stream(act, ST["bo", i], split, lambda: sb_mix(i), None,
                           lambda g, b: norm_hi(2 * i + 1, g, ST["bo", i].g0 + g))
                    res = ST["bo", i]
                else:
                    stream(act, ST["dq", i], split, last[0], last[1])
                    stream(act, ST["dkv", i], split, lambda: norm_y(2 * i))
                    stream(act, ST["uq", i], split, lambda: mla_prep(i))
                    stream(act, ST["ukv", i], split)
                    stream(act, ST["co", i], split, lambda: mla_mix(i), None,
                           lambda g, b: norm_hi(2 * i + 1, g, ST["co", i].g0 + g))
                    res = ST["co", i]
                nu = 2 * i + 1
                st = ST["ff1", i]

                def relu_hi(g, b):
                    act.wait_ge(group_out, g + (st.g0 + 1))
                    act.activation(TMP[:], TMP[:], ACT.Square).then_inc(h_sq, 1)
                    act.wait_ge(h_sq, g + (8 * i + 1))
                    act.activation(HH[:, bass.ds(4 * g, 4), :], TMP[:], ACT.Copy).then_inc(h_hi, 1)

                def ff1_after(g, b):
                    if isinstance(g, int) and g == 0:
                        norm_y(nu)
                    relu_hi(g, b)

                stream(act, st, split, lambda: norm_hi(nu, 1, res.g0 + 1), None, ff1_after, None, loop=True)
                fin = i == DEPTH - 1
                stream(act, ST["ff2", i], split, lambda: relu_hi(7, 1), None,
                       None if fin else lambda g, b: norm_hi(nu + 1, g, ST["ff2", i].g0 + g))
                last[:] = [lambda nu=nu, g=ST["ff2", i].g0 + 1: norm_hi(nu + 1, 1, g), None]
            norm_y(2 * DEPTH)
            for x in range(6):
                tb, half = divmod(x, 2)
                n = TBS[tb][2]
                act.wait_ge(yo_done, x + 1)
                act.activation(YO[0:n, tb, 512 * half:512 * (half + 1)], PS[0:n, (0, 1, 2, 3, 6, 7)[x], :], ACT.Copy) \
                   .then_inc(yo_out, 1)

        @block.vector
        def _(dve):
            own = [0]

            def link(ins):
                own[0] += 1
                ins.then_inc(dve_own, 1)
                dve.wait_ge(dve_own, own[0])

            def over4(ap, n=4):
                return ap.unsqueeze(1).to_broadcast([P, n, ap.shape[-1]])

            def split(st, j, c):
                if st.upt == 2:
                    if j is None:
                        j, c = divmod(c, 8)
                    w = WIDTH.get(st.name, 512)
                    dve.wait_ge(weight_hi, 8 * j + (st.u0 + c + 1))
                    dve.tensor_tensor(WLO[:, c % SPL, 0:w], RAWT[:, c // 2, (c % 2) * w:(c % 2 + 1) * w],
                                      WHI[:, c % SPL, 0:w].bitcast(F32), ALU.subtract).then_inc(weight_lo, 1)
                else:
                    t, k = divmod(c, 3)
                    s = (st.u0 + c) % SPL
                    dve.wait_ge(weight_hi, st.u0 + c + 1)
                    dve.tensor_tensor(WLO[:, s, 0:192], RAWT[:, t % RAW, 192 * k:192 * (k + 1)],
                                      WHI[:, s, 0:192].bitcast(F32), ALU.subtract).then_inc(weight_lo, 1)

            def residual(st, g):
                dve.wait_ge(unit_done, st.done(g))
                dve.tensor_tensor(X[:, 4 * g:4 * g + 4, :], X[:, 4 * g:4 * g + 4, :], PS[:, 4 * g:4 * g + 4, 0:T],
                                  ALU.add).then_inc(group_out, 1)

            def norm_lo(nu, half):
                dve.wait_ge(xg_hi, 2 * nu + half + 1)
                for f in range(4 * half, 4 * half + 4):
                    ins = dve.scalar_tensor_tensor(XGL[:, f, :], X[:, f, :], COLS[:, gain(nu) + f:gain(nu) + f + 1],
                                                   XGH[:, f, :].bitcast(F32), ALU.mult, ALU.subtract)
                ins.then_inc(xg_lo, 1)

            def newton(out, v, y, t):
                link(dve.scalar_tensor_tensor(t, y, 1.0, y, ALU.mult, ALU.mult))
                link(dve.scalar_tensor_tensor(t, t, -0.5, v, ALU.mult, ALU.mult))
                link(dve.scalar_tensor_tensor(out, t, 1.5, y, ALU.add, ALU.mult))

            def rstd(nu):
                dve.wait_ge(stat_done, nu + 1)
                dve.tensor_scalar(NV[:].rearrange("p (a t) -> p a t", a=2), PS[:, 4:6, T:T + T // 2], 1.0 / D, EPS,
                                  ALU.mult, ALU.add).then_inc(var_out, 1)
                dve.wait_ge(y_out, nu + 1)
                newton(RSTD[:], NV[:], NY[:], NT[:])

            dve.wait_ge(xpose_done, 1)
            for slot in range(5):
                n = (77, 112, 112, 64, 64)[slot]
                c0 = (0, cols_a(0), cols_a(1), cols_s(0), cols_s(1))[slot]
                link(dve.tensor_copy(COLS[:, c0:c0 + n], PS[:, slot, 0:n]))
            for half in range(2):
                dve.wait_ge(xpose_done, 2 + half)
                dve.tensor_copy(X[:, 4 * half:4 * half + 4, :], PS[:, 4 * half:4 * half + 4, 0:T]) \
                   .then_inc(group_out, 1)
                norm_lo(0, half) if half == 0 else None
            last = [lambda: None, lambda: norm_lo(0, 1)]

            def mlstm_up(i, la):
                st = ST["up", i]

                def after(g, b):
                    k = 4 * la + g
                    bank = PS[:, 4 * b:4 * b + 4, :]
                    if g == 0:
                        rstd(2 * i)
                    dve.wait_ge(unit_done, st.done(g))
                    if g < 4:
                        if k:
                            dve.wait_ge(xm_lo, k)
                        dve.memset(TMPX[:, :, 0:3], 0.0)
                        c0 = cols_s(la) + CST
                        dve.tensor_copy(TMPX[:, :, 259:262],
                                        COLS[:, c0:c0 + 48].rearrange("p (j b) -> p b j", j=3)[:, 4 * g:4 * g + 4, :])
                        dve.tensor_tensor(TMPX[:, :, 3:259], bank[:, :, 0:TP], over4(RSTD[:, 0:TP]), ALU.mult)
                        link(dve.tensor_tensor(TMPX[:, :, 262:294], bank[:, :, TP:T], over4(RSTD[:, TP:T]), ALU.mult))
                        for s, c in ((0, 256), (1, 291)):
                            ins = dve.tensor_copy(CVO[:, s, :, 4 * g:4 * g + 4].rearrange("p j b -> p b j"),
                                                  TMPX[:, :, c:c + 3])
                        ins.then_inc(group_out, 1)
                    else:
                        if g == 4:
                            dve.wait_ge(xm_lo, 4 * la + 4)
                        else:
                            dve.wait_ge(sigz_out, k - 4)
                        dve.tensor_tensor(TMP[:], bank[:, :, 0:T], over4(RSTD[:]), ALU.mult).then_inc(group_out, 1)

                def late(g):
                    if g < 4:
                        k = 4 * la + g
                        dve.wait_ge(conv_first, k + 1)
                        for j in range(1, 4):
                            for a in range(4):
                                w0 = cols_a(la) + CONVW + AB * j + 4 * g + a
                                ins = dve.scalar_tensor_tensor(CV_[:, a, 0:291], TMPX[:, a, j:j + 291],
                                                               COLS[:, w0:w0 + 1], CV_[:, a, 0:291], ALU.mult, ALU.add)
                            if j < 3:
                                link(ins)
                        ins.then_inc(conv_done, 1)

                stream(dve, st, split, last[0], last[1], after, late)
                last[:] = [lambda: after(7, 1), None]

            def mlstm_qkv(i, la):
                st = ST["qkv", i]

                def after(x, b):
                    h, m = divmod(x, 3)
                    dve.wait_ge(unit_done, st.done(x))
                    bank = PS[:, 4 * b:4 * b + 4, 0:T]
                    if m == 1:
                        ins = dve.tensor_scalar(KT[:, 4 * h:4 * h + 4, :], bank, float(ADH) ** -0.5, None, ALU.mult)
                    else:
                        ins = dve.tensor_copy((QT if m == 0 else VT_)[:, 4 * h:4 * h + 4, :], bank)
                    ins.then_inc(group_out, 1)

                stream(dve, st, split, last[0], None, after)
                return lambda: after(11, 1)

            def mlstm_mix(i, la, evac_last):
                evac_last()
                dve.wait_ge(gates_done, la + 1)
                dve.tensor_copy(G8[:], PS[0:8, 0, 0:T]).then_inc(g8_out, 1)
                dve.wait_ge(gsel_done, la + 1)
                F, E, B, A = (ROWS[:, r, :] for r in range(4))
                link(dve.tensor_scalar(F, PS[0:4, 2, 0:T], SMALL[:, 2 + la:3 + la], None, ALU.add))
                link(dve.tensor_scalar(B, F, 0.0, None, ALU.max))
                dve.scalar_tensor_tensor(E, B, -2.0, F, ALU.mult, ALU.add).then_inc(f_out, 1)
                dve.wait_ge(fabs_out, la + 1)
                link(dve.scalar_tensor_tensor(F, F, 0.0, E, ALU.min, ALU.subtract))
                link(dve.tensor_tensor_scan(B[:, 0:TP], F[:, 0:TP], F[:, 0:TP], 0.0, ALU.add, ALU.bypass))
                link(dve.tensor_tensor_scan(B[:, TP:T], F[:, TP:T], F[:, TP:T], 0.0, ALU.add, ALU.bypass))
                link(dve.scalar_tensor_tensor(A, PS[0:4, 1, 0:T], SMALL[:, la:la + 1], B, ALU.add, ALU.subtract))
                link(dve.tensor_tensor_scan(E[:, 0:TP], A[:, 0:TP], A[:, 0:TP], 0.0, ALU.max, ALU.max))
                link(dve.tensor_tensor_scan(E[:, TP:T], A[:, TP:T], A[:, TP:T], SMALL[:, 4 + la:5 + la],
                                            ALU.max, ALU.max))
                link(dve.tensor_scalar(R[:, 0:T], E, -1.0, None, ALU.mult))
                link(dve.tensor_tensor(R[:, T:2 * T], R[:, 0:T], B, ALU.subtract))
                dve.tensor_scalar(R[:, 2 * T:2 * T + TS], R[:, TP:T], SMALL[:, 4 + la:5 + la], None,
                                  ALU.add).then_inc(rows_out, 1)
                if la:
                    dve.wait_ge(m_dma, 32 * la)
                dve.tensor_scalar(SMALL[:, 6:7], R[:, T + TP - 1:T + TP], -1.0, None, ALU.mult)
                dve.tensor_scalar(SMALL[:, 7:8], R[:, 2 * T - 1:2 * T], -1.0, None, ALU.mult).then_inc(m_out, 1)
                dve.wait_ge(acol_done, la + 1)
                dve.tensor_copy(ACOL[:, 0:2, :], PS[:, 3, 128:136].rearrange("p (a h) -> p a h", a=2))
                link(dve.tensor_copy(ACOL[0:TS, 2, :], PS[0:TS, 3, 136:140]))
                dve.wait_ge(vxp_out, 12 * (la + 1))

                def decay(h):
                    U = AH * la + h
                    dve.wait_ge(bcast_done, U + 1)
                    dve.tensor_scalar(DT[:, 0:256], PS[:, 0, 0:256], ACOL[:, 0, h:h + 1], 0.0, ALU.add, ALU.min)
                    dve.tensor_scalar(DT[:, 256:384], PS[:, 0, 128:256], ACOL[:, 1, h:h + 1], 0.0, ALU.add, ALU.min)
                    dve.tensor_scalar(DT[0:TS, 384:416], PS[0:TS, 0, 256:288], ACOL[0:TS, 2, h:h + 1], 0.0,
                                      ALU.add, ALU.min).then_inc(darg_out, 1)
                    dve.wait_ge(em_out, U + 1)
                    link(dve.tensor_tensor(QW[:, 0], QT[:, 4 * h:4 * h + 4, TP:T], over4(WB[:, h % 2, :]), ALU.mult))
                    n0 = cols_s(la) + N0 + 4 * h
                    dve.tensor_tensor(QW[:, 1], QW[:, 0], COLS[:, n0:n0 + 4].unsqueeze(2).to_broadcast([P, 4, TS]),
                                      ALU.mult).then_inc(qw_out, 1)
                    dve.wait_ge(dmask_out, U + 1)
                    dve.wait_ge(score_done, U + 1)
                    dve.tensor_tensor(PT_[:, 0:384], PS[:, 2, 0:384], DT[:, 0:384], ALU.mult)
                    dve.tensor_tensor(PT_[0:TS, 384:416], PS[0:TS, 2, 384:416], DT[0:TS, 384:416], ALU.mult) \
                       .then_inc(prob_out, 1)

                def keys(h):
                    U = AH * la + h
                    dve.wait_ge(kxp_done, U + 1)
                    dve.tensor_scalar(KG[:, 0, :], PS[:, 4, :], DT[:, 255:256], None, ALU.mult)
                    dve.tensor_scalar(KG[:, 1, :], PS[:, 5, :], DT[:, 383:384], None, ALU.mult)
                    dve.tensor_scalar(KG[0:TS, 2, :], PS[0:TS, 6, :], DT[0:TS, 415:416], None, ALU.mult) \
                       .then_inc(kg_out, 1)

                decay(0)
                keys(0)
                for h in range(AH):
                    U = AH * la + h
                    gs = WB[:, h % 2, TS - 1:TS]
                    H4 = slice(4 * h, 4 * h + 4)
                    dve.wait_ge(num_done, U + 1)
                    link(dve.scalar_tensor_tensor(EM[:], PS[:, 3, 0:T], -1.0, EM[:], ALU.mult, ALU.max))
                    link(dve.tensor_tensor(EM[:], PS[:, 3, 0:T], EM[:], ALU.max))
                    link(dve.reciprocal(EM[:], EM[:]))
                    dve.tensor_tensor(HB[:], PS[:, 4:8, 0:T], over4(EM[:]), ALU.mult).then_inc(hnum_out, 1)
                    if h + 1 < AH:
                        decay(h + 1)
                    dve.wait_ge(n_done, U + 1)
                    dve.tensor_copy(NOUT[:, 0, H4], PS[:, 3, 300:304])
                    n0 = cols_s(la) + N0 + 4 * h
                    dve.scalar_tensor_tensor(NOUT[:, 1, H4], COLS[:, n0:n0 + 4], gs, PS[:, 3, 304:308],
                                             ALU.mult, ALU.add).then_inc(n_out, 1)
                    dve.wait_ge(mean_done, U + 1)
                    dve.wait_ge(hnum_out, U + 1)
                    dve.scalar_tensor_tensor(HB[:], over4(PS[:, 3, 0:T]), -1.0 / ADH, HB[:], ALU.mult, ALU.add) \
                       .then_inc(hc_out, 1)
                    for b in range(4):
                        dve.wait_ge(cs_done, 4 * U + b + 1)
                        ins = dve.scalar_tensor_tensor(C0[:, h % 2, b, :], C0[:, h % 2, b, :], gs, PS[:, 4 + b, :],
                                                       ALU.mult, ALU.add)
                    ins.then_inc(cs_out, 1)
                    dve.wait_ge(hvar_done, U + 1)
                    V, Y, N, RS = (KT[:, 4 * h + x, :] for x in range(4))
                    dve.tensor_scalar(V, PS[:, 3, 0:T], 1.0 / ADH, EPS, ALU.mult, ALU.add).then_inc(hv_out, 1)
                    if h + 1 < AH:
                        keys(h + 1)
                    dve.wait_ge(hy_out, U + 1)
                    newton(RS, V, Y, N)
                    dve.wait_ge(hc_out, U + 1)
                    link(dve.tensor_tensor(HB[:], HB[:], over4(RS), ALU.mult))
                    dve.wait_ge(sx_out, U + 1)
                    for a in range(4):
                        g0 = cols_a(la) + GHEAD + 4 * h + a
                        ins = dve.scalar_tensor_tensor(HB[:, a, :], HB[:, a, :], COLS[:, g0:g0 + 1], SX[:, a, :],
                                                       ALU.mult, ALU.add)
                    link(ins)
                    dve.tensor_tensor(HB[:], HB[:], SIGZ[:, H4, :], ALU.mult).then_inc(mo_out, 1)
                    dve.wait_ge(mh_hi, U + 1)
                    dve.tensor_tensor(HL[:, H4, :], HB[:], HH[:, H4, :].bitcast(F32), ALU.subtract).then_inc(mh_lo, 1)

            def sb_mix(i, evac_last):
                evac_last()
                for s in range(BH + 4):
                    h = s
                    if h < BH:
                        dve.wait_ge(bz_done, h + 1)
                        if h >= 3:
                            dve.wait_ge(bs_done, h - 2)
                        link(dve.tensor_scalar(BSP[:, h % 3, :], PS[:, h % 5, 0:SBW], 0.0, None, ALU.max))
                        dve.scalar_tensor_tensor(BE[:, h % 3, :], BSP[:, h % 3, :], -2.0, PS[:, h % 5, 0:SBW],
                                                 ALU.mult, ALU.add).then_inc(babs_out, 1)
                    h = s - 1
                    if 0 <= h < BH:
                        dve.wait_ge(be_out, h + 1)
                        dve.tensor_tensor(BSP[:, h % 3, :], BSP[:, h % 3, :], BE[:, h % 3, :], ALU.add) \
                           .then_inc(bsp_out, 1)
                    h = s - 2
                    if 0 <= h < BH:
                        dve.wait_ge(bs_done, h + 1)
                        if h >= 3:
                            dve.wait_ge(bo_done, h - 2)
                        dve.tensor_scalar(BATT[:, h % 3, :], PS[:, h % 5, 0:SBW], 0.0, None, ALU.min) \
                           .then_inc(bt_out, 1)
                    h = s - 4
                    if h >= 0 and h % 2:
                        dve.wait_ge(bo_hi, h // 2 + 1)
                        dve.tensor_tensor(HL[:, h // 2, :], PS[:, 5 + h // 2 % 2, 0:T],
                                          HH[:, h // 2, :].bitcast(F32), ALU.subtract).then_inc(bo_lo, 1)

            def sb_qkv(i):
                st = ST["bqkv", i]

                def after(x, b):
                    if x == 0:
                        rstd(2 * i)
                    dve.wait_ge(unit_done, st.done(x))
                    bank = PS[:, 4 * b:4 * b + 4, 0:T]
                    m, half = divmod(x, 2)
                    if m == 0:
                        ins = dve.scalar_tensor_tensor(BQ[:, 4 * half:4 * half + 4, :], bank, float(BDH) ** -0.5,
                                                       over4(RSTD[:]), ALU.mult, ALU.mult)
                    else:
                        dst = (BK if m == 1 else BV)[:, 4 * half:4 * half + 4, 0:T]
                        ins = dve.tensor_tensor(dst, bank, over4(RSTD[:]), ALU.mult)
                    ins.then_inc(group_out, 1)

                stream(dve, st, split, last[0], last[1], after)
                return lambda: after(5, 1)

            def mla_first(i):
                dve.wait_ge(unit_done, ST["dq", i].u1)
                rstd(2 * i)
                dve.tensor_tensor(CQF[:], PS[:, 0:3, 0:T], over4(RSTD[:], 3), ALU.mult).then_inc(group_out, 1)

            def mla_prep(i):
                dve.wait_ge(unit_done, ST["dkv", i].u1)
                for b in range(2):
                    dve.wait_ge(cp_dma[b], 16 * 8)
                dve.tensor_tensor(CKF[:], PS[:, 4:6, 0:T], over4(RSTD[:], 2), ALU.mult)
                dve.tensor_tensor(CKR_[:], PS[0:32, 6, 0:T], RSTD[0:32, :], ALU.mult).then_inc(group_out, 1)
                dve.wait_ge(cstat_done, 1)
                dve.tensor_scalar(CV3[:, 0, 0, :], PS[:, 0, 0:T], 1.0 / CQR, EPS, ALU.mult, ALU.add)
                dve.tensor_scalar(CV3[:, 0, 1, :], PS[:, 1, 0:T], 1.0 / CKR, EPS, ALU.mult, ALU.add) \
                   .then_inc(cv_out, 1)
                dve.wait_ge(c_in, 16 * 7)
                link(dve.tensor_tensor(KRT[:], PS[0:32, 3, 0:T], KROPE[:, 1, :], ALU.mult))
                link(dve.tensor_tensor(CKRO[:, 0:T], CKR_[:], KROPE[:, 0, :], ALU.mult))
                dve.tensor_tensor(CKRO[:, 0:T], CKRO[:, 0:T], KRT[:], ALU.add)
                dve.tensor_copy(CKRO[:, T:TK], PS[0:32, 2, 256:384]).then_inc(kro_out, 1)
                dve.wait_ge(cy_out, 1)
                v, y, t = (CV3[:, x].rearrange("p a t -> p (a t)") for x in range(3))
                newton(CRST[:].rearrange("p a t -> p (a t)"), v, y, t)
                dve.tensor_copy(CKV[:, :, T:TK], PS[:, 2, 0:256].rearrange("p (a t) -> p a t", a=2))
                for b in range(2):
                    ins = dve.scalar_tensor_tensor(CKV[:, b, 0:T], CKF[:, b, :], COLS[:, GKV + b:GKV + b + 1],
                                                   CRST[:, 1, :], ALU.mult, ALU.mult)
                ins.then_inc(ckv_out, 1)
                dve.wait_ge(cq_hi, 1)
                for b in range(3):
                    ins = dve.scalar_tensor_tensor(CQL[:, b, :], CQF[:, b, :], COLS[:, GQ + b:GQ + b + 1],
                                                   CQH[:, b, :].bitcast(F32), ALU.mult, ALU.subtract)
                ins.then_inc(cq_lo, 1)
                dve.wait_ge(ck_hi, 1)
                dve.tensor_tensor(CKL[:], CKV[:], CKH[:].bitcast(F32), ALU.subtract).then_inc(ck_lo, 1)

            def uq_out(g, b):
                st = ST["uq", 2]
                dve.wait_ge(unit_done, st.done(g))
                dve.tensor_tensor(CQ96[:, 2 * g:2 * g + 2, :], PS[0:CQD, 4 * b:4 * b + 2, 0:T],
                                  CRST[0:CQD, 0, :].unsqueeze(1).to_broadcast([CQD, 2, T]), ALU.mult) \
                   .then_inc(group_out, 1)

            def rotate(g, b):
                cos, sin = (COSS[:, x, :].unsqueeze(1).to_broadcast([CQD, 2, T]) for x in range(2))
                dve.wait_ge(rot_done, g + 1)
                rot = PS[0:CQD, 4 * b + 2:4 * b + 4, 0:T]
                link(dve.tensor_tensor(CQ96[:, 2 * g:2 * g + 2, :], CQ96[:, 2 * g:2 * g + 2, :], cos, ALU.mult))
                t = CSQ[0:CQD, 0:2, :]
                link(dve.tensor_tensor(t, rot, sin, ALU.mult))
                dve.tensor_tensor(CQ96[:, 2 * g:2 * g + 2, :], CQ96[:, 2 * g:2 * g + 2, :], t, ALU.add) \
                   .then_inc(rot_out, 1)

            def ukv_out(g):
                t, m = divmod(g, 2)
                if m == 0:
                    dve.wait_ge(ukv_done, t + 1)
                    dve.tensor_copy(CK96[0:64, 4 * t:4 * t + 4, :], PS[0:64, 0:4, 0:TK]).then_inc(group_out, 1)
                else:
                    dve.wait_ge(unit_done, ST["ukv", 2].u0 + 2 * (t + 1))
                    dve.tensor_copy(CVT[:, 0:3, 256 * t:256 * (t + 1)], PS[:, 4:7, 0:256])
                    dve.tensor_copy(CVT[0:TS, 3, 256 * t:256 * (t + 1)], PS[0:TS, 7, 0:256]).then_inc(group_out, 1)

            def mla_mix(i):
                ukv_out(7)
                for s in range(CH + 3):
                    h = s
                    if h < CH and h % 4 == 0:
                        g = h // 4
                        dve.wait_ge(ss_sc, g + 1)
                        if g:
                            dve.wait_ge(ss_xp, g)
                        link(dve.reduce_max(CSTS[:, 0:1], PS[:, 6, 0:160], AX_X))
                        dve.tensor_scalar(CSTS[:, 1:2], CSTS[:, 0:1], -CSCALE, None, ALU.mult).then_inc(ss_max, 1)
                        dve.wait_ge(ss_exp, g + 1)
                        link(dve.reciprocal(CSTS[:, 3:4], CSTS[:, 2:3]))
                        dve.tensor_scalar(CPS[:], CPS[:], CSTS[:, 3:4], None, ALU.mult).then_inc(ss_nrm, 1)
                    if h < CH:
                        c = CST_[:, h % 2]
                        dve.wait_ge(cs_sc, h + 1)
                        dve.reduce_max(c[:, 0, 0:1], PS[:, h % 2, 0:128], AX_X)
                        link(dve.reduce_max(c[:, 0, 1:2], PS[:, h % 2, 128:384], AX_X))
                        dve.tensor_scalar(c[:, 1, :], c[:, 0, :], -CSCALE, None, ALU.mult).then_inc(c_max, 1)
                    h = s - 1
                    if 0 <= h < CH:
                        c = CST_[:, h % 2]
                        dve.wait_ge(c_exp, h + 1)
                        link(dve.reciprocal(c[:, 3, :], c[:, 2, :]))
                        dve.tensor_scalar(PB[:, h % 2, 0:128], PB[:, h % 2, 0:128], c[:, 3, 0:1], None, ALU.mult)
                        dve.tensor_scalar(PB[:, h % 2, 128:384], PB[:, h % 2, 128:384], c[:, 3, 1:2], None,
                                          ALU.mult).then_inc(c_nrm, 1)
                    h = s - 3
                    if h >= 0 and h % 2:
                        dve.wait_ge(c_ohi, h // 2 + 1)
                        dve.tensor_tensor(HL[:, h // 2, :], PS[:, 4 + h // 2 % 2, 0:T],
                                          HH[:, h // 2, :].bitcast(F32), ALU.subtract).then_inc(c_olo, 1)

            for i in range(DEPTH):
                la = i // 3
                nu = 2 * i + 1
                if i % 3 == 0:
                    mlstm_up(i, la)
                    evac_last = mlstm_qkv(i, la)
                    res = ST["down", i]
                    mix = lambda: mlstm_mix(i, la, evac_last)
                elif i % 3 == 1:
                    evac_last = sb_qkv(i)
                    res = ST["bo", i]
                    mix = lambda: sb_mix(i, evac_last)
                else:
                    stream(dve, ST["dq", i], split, last[0], last[1])
                    stream(dve, ST["dkv", i], split, lambda: mla_first(i))

                    def uq_after(g, b):
                        uq_out(g, b)
                        if g:
                            rotate(g - 1, b ^ 1)

                    stream(dve, ST["uq", i], split, lambda: mla_prep(i), None, uq_after)

                    def ukv_first():
                        uq_out(7, 1)
                        rotate(6, 0)
                        rotate(7, 1)

                    st = ST["ukv", i]
                    for u in range(8):
                        split(st, None, u)
                        if u == 2:
                            ukv_first()
                        if u in (3, 5, 7):
                            ukv_out(u - 3)
                            ukv_out(u - 2)
                    res = ST["co", i]
                    mix = lambda: (ukv_out(6), mla_mix(i))
                stream(dve, res, split, mix, None, lambda g, b: residual(res, g), lambda g: norm_lo(nu, g))
                st = ST["ff1", i]

                def ff1_after(g, b):
                    if isinstance(g, int) and g == 0:
                        rstd(nu)
                        if i % 3 == 0:
                            dve.wait_ge(nst_dma, 32 * (la + 1))
                    dve.wait_ge(unit_done, 8 * g + (st.u0 + 8))
                    dve.scalar_tensor_tensor(TMP[:], PS[:, 4 * b:4 * b + 4, 0:T], 0.0, over4(RSTD[:]),
                                             ALU.max, ALU.mult).then_inc(group_out, 1)

                def ff1_late(g):
                    if isinstance(g, int) and g == 0:
                        for s, n in (((cs_dma[0], 32 * (la + 1)), (cs_dma[1], 32 * (la + 1))),
                                     ((b_dma, 64),), ((c_dma, 64),))[i % 3]:
                            dve.wait_ge(s, n)
                    dve.wait_ge(h_hi, g + (8 * i + 1))
                    dve.tensor_tensor(HL[:, bass.ds(4 * g, 4), :], TMP[:], HH[:, bass.ds(4 * g, 4), :].bitcast(F32),
                                      ALU.subtract).then_inc(h_lo, 1)

                stream(dve, st, split, lambda: residual(res, 1), lambda: norm_lo(nu, 1), ff1_after, ff1_late,
                       loop=True)
                ff2 = ST["ff2", i]
                fin = i == DEPTH - 1
                stream(dve, ff2, split, lambda: ff1_after(7, 1), lambda: ff1_late(7),
                       lambda g, b: residual(ff2, g), None if fin else lambda g: norm_lo(nu + 1, g))
                last[:] = [lambda ff2=ff2: residual(ff2, 1), lambda nu=nu: norm_lo(nu + 1, 1)]
            last[0]()
            rstd(2 * DEPTH)
            for f in range(DB):
                ins = dve.scalar_tensor_tensor(YF[:, f, :], X[:, f, :], COLS[:, NFIN + f:NFIN + f + 1], RSTD[:],
                                               ALU.mult, ALU.mult)
            ins.then_inc(yf_out, 1)

        @block.gpsimd
        def _(pool):
            own = [0]

            def link(ins):
                own[0] += 1
                ins.then_inc(pool_own, 1)
                pool.wait_ge(pool_own, own[0])

            def squares(nu, half, g, done=None):
                pool.wait_ge(group_out, g + 1)
                if nu or half:
                    pool.wait_ge(ssum, 2 * nu + half)
                x = X[:, 4 * half:4 * half + 4, :]
                link(pool.tensor_tensor(SQ[:], x, x, ALU.mult))
                link(pool.tensor_tensor(SQ[:, 0:2, :], SQ[:, 0:2, :], SQ[:, 2:4, :], ALU.add))
                pool.tensor_tensor(SSUM[:, half, :], SQ[:, 0, :], SQ[:, 1, :], ALU.add).then_inc(ssum, 1)

            squares(0, 0, 0)
            squares(0, 1, 1)
            for i in range(DEPTH):
                la = i // 3
                if i % 3 == 0:
                    for g in range(4):
                        k = 4 * la + g
                        pool.wait_ge(xm_hi, k + 1)
                        s = slice(16 + 4 * g, 20 + 4 * g)
                        pool.tensor_tensor(HL[:, s, 0:TP], TMPX[:, :, 3:3 + TP], HH[:, s, 0:TP].bitcast(F32),
                                           ALU.subtract)
                        pool.tensor_tensor(HL[:, s, TP:T], TMPX[:, :, 262:294], HH[:, s, TP:T].bitcast(F32),
                                           ALU.subtract).then_inc(xm_lo, 1)
                        pool.wait_ge(xc_hi, k + 1)
                        s = slice(4 * g, 4 * g + 4)
                        pool.tensor_tensor(HL[:, s, :], XCF[:], HH[:, s, :].bitcast(F32), ALU.subtract) \
                            .then_inc(xc_lo, 1)

                    def dmask(h):
                        pool.wait_ge(dexp_out, AH * la + h + 1)
                        if h == 0:
                            pool.wait_ge(mask_in, 16 * (la + 1))
                        pool.tensor_tensor(DT[:, 0:384], DT[:, 0:384], MASKM[:, 0:384], ALU.mult)
                        pool.tensor_tensor(DT[0:TS, 384:416], DT[0:TS, 384:416], MASKM[0:TS, 384:416], ALU.mult) \
                            .then_inc(dmask_out, 1)

                    dmask(0)
                    for h in range(AH):
                        if h:
                            pool.wait_ge(mo_out, AH * la + h)
                        H4 = slice(4 * h, 4 * h + 4)
                        link(pool.tensor_tensor(SX[:], HH[:, H4, :].bitcast(F32), HL[:, H4, :].bitcast(F32), ALU.add))
                        for a in range(4):
                            s0 = cols_a(la) + SKIP + 4 * h + a
                            ins = pool.tensor_scalar(SX[:, a, :], SX[:, a, :], COLS[:, s0:s0 + 1], None, ALU.mult)
                        ins.then_inc(sx_out, 1)
                        if h + 1 < AH:
                            dmask(h + 1)
                    res = ST["down", i]
                elif i % 3 == 1:
                    pool.wait_ge(group_out, ST["bqkv", i].g0 + 1)
                    pool.memset(BK[:, :, T:384], 0.0).then_inc(bpad, 1)
                    pool.wait_ge(b_in, 16 * 5)
                    for s in range(BH + 2):
                        h = s
                        if h < BH:
                            pool.wait_ge(bsp_out, h + 1)
                            pool.tensor_tensor(BSP[:, h % 3, :], BSP[:, h % 3, :], BMASK[:], ALU.mult) \
                                .then_inc(bspm_out, 1)
                        h = s - 2
                        if h >= 0:
                            pool.wait_ge(batt_out, h + 1)
                            pool.tensor_tensor(BATT[:, h % 3, :], BATT[:, h % 3, :], BMASK[:], ALU.mult) \
                                .then_inc(battm_out, 1)
                    res = ST["bo", i]
                else:
                    pool.wait_ge(group_out, ST["dq", i].g1)
                    link(pool.tensor_tensor(CSQ[:], CQF[:], CQF[:], ALU.mult))
                    link(pool.tensor_tensor(CSQ[:, 0, :], CSQ[:, 0, :], CSQ[:, 1, :], ALU.add))
                    link(pool.tensor_tensor(CSS[:, 0, :], CSQ[:, 0, :], CSQ[:, 2, :], ALU.add))
                    pool.wait_ge(group_out, ST["dkv", i].g1)
                    link(pool.tensor_tensor(CSQ[:, 0:2, :], CKF[:], CKF[:], ALU.mult))
                    pool.tensor_tensor(CSS[:, 1, :], CSQ[:, 0, :], CSQ[:, 1, :], ALU.add).then_inc(css_out, 1)
                    res = ST["co", i]
                for half in range(2):
                    squares(2 * i + 1, half, res.g0 + half)
                for half in range(2):
                    squares(2 * i + 2, half, ST["ff2", i].g0 + half)

        @block.tensor
        def _(pe):
            def mm(out, lhsT, rhs, start=True, stop=True, **kw):
                return pe.matmul(out, lhsT, rhs, start=start, stop=stop, **kw)

            def xp(out, in_):
                n = in_.shape[0]
                return pe.transpose(out, in_, IDENT[0:n, 0:n])

            def kblock(t, k):
                return t[:, bass.ds(k, 1), :].rearrange("p a t -> p (a t)") if not isinstance(k, int) else t[:, k, :]

            def unit(u, slot, b, cols, rh, rl, start, stop):
                pe.wait_ge(weight_lo, u + 1)
                for a, (c, m) in enumerate(cols):
                    out = PS[0:m, 4 * b + a, 0:rh.shape[-1]]
                    mm(out, WHI[:, slot, c:c + m], rh, start, False)
                    mm(out, WHI[:, slot, c:c + m], rl, False, False)
                    ins = mm(out, WLO[:, slot, c:c + m], rh, False, stop)
                ins.then_inc(unit_done, 1)

            FOUR = [(P * a, P) for a in range(4)]

            def banks_free(st, g):
                pe.wait_ge(group_out, g + (st.g0 - 1))

            def xg_group(st, g, b, nu=None, cols=FOUR):
                banks_free(st, g)
                for k in range(DB):
                    if nu is not None and k % 4 == 0:
                        pe.wait_ge(xg_lo, 2 * nu + k // 4 + 1)
                    unit(8 * g + (st.u0 + k), k % SPL, b, cols, XGH[:, k, :], XGL[:, k, :], k == 0, k == DB - 1)

            def stat(nu, evacuated):
                pe.wait_ge(ssum, 2 * nu + 2)
                pe.wait_ge(group_out, evacuated)
                for c in range(2):
                    for half in range(2):
                        ins = mm(PS[:, 4 + c, T:T + T // 2], ONES[:], SSUM[:, half, c * T // 2:(c + 1) * T // 2],
                                 half == 0, half == 1)
                ins.then_inc(stat_done, 1)
                pe.wait_ge(var_out, nu + 1)

            def xg_stage(st, nu):
                xg_group(st, 0, 0, nu)
                stat(nu, st.g0)
                xg_group(st, 1, 1)
                with pe.Fori(1, st.groups // 2) as q:
                    xg_group(st, 2 * q, 0)
                    xg_group(st, 2 * q + 1, 1)

            def hh_stage(st, ready):
                for g in range(2):
                    banks_free(st, g)
                    for k in range(st.upg):
                        if g == 0:
                            ready(k)
                        unit(st.u0 + st.upg * g + k, k % SPL, g, FOUR, HH[:, k, :], HL[:, k, :],
                             k == 0, k == st.upg - 1)

            pe.wait_ge(const_in, 32)
            pe.wait_ge(rows_in, 16 * 23)
            for slot in range(5):
                n = (77, 112, 112, 64, 64)[slot]
                ins = xp(PS[:, slot, 0:n], VROWS[0:n, slot, :])
            ins.then_inc(xpose_done, 1)
            pe.wait_ge(dve_own, 5)
            pe.wait_ge(x_in, 32)
            for half in range(2):
                for f in range(4 * half, 4 * half + 4):
                    for tb, t0, n in TBS:
                        ins = xp(PS[:, f, t0:t0 + n], XIN[0:n, tb, f * P:(f + 1) * P])
                ins.then_inc(xpose_done, 1)

            def mlstm_mix(i, la):
                st = ST["qkv", i]
                pe.wait_ge(group_out, st.g1)
                pe.wait_ge(mconst_in, 16 * (la + 1))
                for x in range(48):
                    m, f = divmod(x, AB)
                    ins = mm(PS[0:8, 0, 0:T], WG[:, x, :], (QT, KT, VT_)[m][:, f, :], x == 0, x == 47)
                ins.then_inc(gates_done, 1)
                xp(PS[0:96, 3, 0:P], CVO[:].rearrange("p s j b -> p (s j b)")).then_inc(cvs_done, 1)

                def v_tokens(x):
                    h, tb = divmod(x, 3)
                    _, t0, n = TBS[tb]
                    if x >= 4:
                        pe.wait_ge(vxp_out, 12 * la + x - 3)
                    for b in range(4):
                        ins = xp(PS[0:n, 4 + x % 4, b * P:(b + 1) * P], VT_[:, 4 * h + b, t0:t0 + n])
                    ins.then_inc(vxp_done, 1)

                for x in range(3):
                    v_tokens(x)
                pe.wait_ge(g8_out, la + 1)
                mm(PS[0:4, 1, 0:T], IDENT[0:8, 0:4], G8[:])
                mm(PS[0:4, 2, 0:T], IDENT[0:8, 4:8], G8[:]).then_inc(gsel_done, 1)
                for x in range(3, 12):
                    v_tokens(x)
                pe.wait_ge(rows_out, la + 1)
                pe.wait_ge(cvs_out, la + 1)
                for tb, t0, n in TBS:
                    ins = xp(PS[0:n, 3, 128 + 4 * tb:132 + 4 * tb], ROWS[:, 3, t0:t0 + n])
                ins.then_inc(acol_done, 1)
                pe.wait_ge(sel_in, 16 * (la + 1))

                def scores(h):
                    U = AH * la + h
                    if h:
                        pe.wait_ge(dexp_out, U)
                        pe.wait_ge(em_out, U)
                    mm(PS[:, 0, 0:T], SEL[:, h, :], R[:, 0:T])
                    mm(PS[:, 1, 0:T + TS], SEL[:, h, :], R[:, T:2 * T + TS]).then_inc(bcast_done, 1)
                    if h:
                        pe.wait_ge(prob_out, U)
                    for o_, m, s0, t0, n in ((0, P, 0, 0, 256), (256, P, P, P, 128), (384, TS, TP, TP, TS)):
                        for b in range(4):
                            f = 4 * h + b
                            ins = mm(PS[0:m, 2, o_:o_ + n], KT[:, f, s0:s0 + m], QT[:, f, t0:t0 + n], b == 0, b == 3)
                    ins.then_inc(score_done, 1)

                def keys(h):
                    U = AH * la + h
                    if h:
                        pe.wait_ge(cs_out, U)
                    else:
                        pe.wait_ge(vxp_out, 12 * (la + 1))
                    for tb, t0, n in TBS:
                        for b in range(4):
                            ins = xp(PS[0:n, 4 + tb, b * P:(b + 1) * P], KT[:, 4 * h + b, t0:t0 + n])
                    ins.then_inc(kxp_done, 1)

                scores(0)
                keys(0)
                for h in range(AH):
                    U = AH * la + h
                    pe.wait_ge(prob_out, U + 1)
                    pe.wait_ge(qw_out, U + 1)
                    pe.wait_ge(kg_out, U + 1)
                    pe.wait_ge(c0_in[h % 2], 16 * (2 * la + h // 2 + 1))
                    if h:
                        pe.wait_ge(hv_out, U)
                        pe.wait_ge(n_out, U)
                    for e in range(5):
                        bank = 3 + e
                        c = slice(512 * h + (e - 1) * P, 512 * h + e * P)
                        v0, v1, v2 = (ONES[:], ONES[:], ONES[0:TS, :]) if e == 0 else \
                            (VTOK[:, 0, c], VTOK[:, 1, c], VTOK[0:TS, 2, c])
                        mm(PS[:, bank, 0:256], v0, PT_[:, 0:256], True, False)
                        mm(PS[:, bank, 128:256], v1, PT_[:, 256:384], False, True)
                        mm(PS[:, bank, 256:288], v2, PT_[0:TS, 384:416], True, False)
                        for b in range(4):
                            old = ONES[:] if e == 0 else C0[:, h % 2, b, (e - 1) * P:e * P]
                            ins = mm(PS[:, bank, 256:288], old, QW[:, 1 if e == 0 else 0, b, :], False, b == 3)
                    ins.then_inc(num_done, 1)
                    if h + 1 < AH:
                        scores(h + 1)
                    pe.wait_ge(hnum_out, U + 1)
                    vh = slice(512 * h, 512 * (h + 1))
                    for b in range(4):
                        kb = slice(b * P, (b + 1) * P)
                        mm(PS[:, 3, 300 + b:301 + b], KG[:, 0, kb], ONES[:, 0:1], True, False)
                        mm(PS[:, 3, 300 + b:301 + b], KG[:, 1, kb], ONES[:, 0:1], False, True)
                    for b in range(4):
                        ins = mm(PS[:, 3, 304 + b:305 + b], KG[0:TS, 2, b * P:(b + 1) * P], ONES[0:TS, 0:1])
                    ins.then_inc(n_done, 1)
                    for b in range(4):
                        kb = slice(b * P, (b + 1) * P)
                        mm(PS[:, 4 + b, :], KG[:, 0, kb], VTOK[:, 0, vh], True, False)
                        mm(PS[:, 4 + b, :], KG[:, 1, kb], VTOK[:, 1, vh], False, True).then_inc(cp_done, 1)
                    pe.wait_ge(n_out, U + 1)
                    for b in range(4):
                        ins = mm(PS[:, 3, 0:T], ONES[:], HB[:, b, :], b == 0, b == 3)
                    ins.then_inc(mean_done, 1)
                    for b in range(4):
                        pe.wait_ge(cp_out, 4 * U + b + 1)
                        mm(PS[:, 4 + b, :], KG[0:TS, 2, b * P:(b + 1) * P], VTOK[0:TS, 2, vh]).then_inc(cs_done, 1)
                    pe.wait_ge(hsq_out, U + 1)
                    for b in range(4):
                        ins = mm(PS[:, 3, 0:T], ONES[:], QT[:, 4 * h + b, :], b == 0, b == 3)
                    ins.then_inc(hvar_done, 1)
                    if h + 1 < AH:
                        keys(h + 1)
                pe.wait_ge(n_out, AH * (la + 1))
                xp(PS[0:32, 0, 0:P], NOUT[:].rearrange("p s f -> p (s f)")).then_inc(nst_done, 1)
                pe.wait_ge(nst_out, la + 1)
                pe.wait_ge(hv_out, AH * (la + 1))
                pe.wait_ge(cs_out, AH * (la + 1))

            def sb_mix(i):
                pe.wait_ge(group_out, ST["bqkv", i].g1)
                pe.wait_ge(b_in, 16 * 5)
                for x in range(14):
                    if x >= 8:
                        pe.wait_ge(bxp_out, x - 7)
                    if x < 2:
                        for b in range(4):
                            f = 4 * x + b
                            ins = xp(PS[:, x % 8, b * P:(b + 1) * P], BKPT[:, f * P:(f + 1) * P])
                    else:
                        kv, y = divmod(x - 2, 6)
                        tb, half = divmod(y, 2)
                        _, t0, n = TBS[tb]
                        for b in range(4):
                            ins = xp(PS[0:n, x % 8, b * P:(b + 1) * P], (BV, BK)[kv][:, 4 * half + b, t0:t0 + n])
                    ins.then_inc(bxp_done, 1)
                pe.wait_ge(bxp_out, 14)
                pe.wait_ge(bpad, 1)
                for s in range(BH + 4):
                    h = s
                    if h < BH:
                        if h >= 5:
                            pe.wait_ge(bt_out, h - 4)
                        r, f = slice(64 * (h % 2), 64 * (h % 2) + 64), h // 2
                        z = PS[:, h % 5, :]
                        mm(z[:, 0:256], BK[r, f, 0:P], BQ[r, f, 0:TP], True, True, skip_group_check=True)
                        mm(z[:, 256:384], BK[r, f, P:TP], BQ[r, f, P:TP], False, True, skip_group_check=True)
                        mm(z[:, 384:416], BKP[r, f, :], BQ[r, f, TP:T], False, True, skip_group_check=True)
                        mm(z[:, 416:448], BK[r, f, TP:384], BQ[r, f, TP:T], False, True, skip_group_check=True) \
                            .then_inc(bz_done, 1)
                    h = s - 2
                    if 0 <= h < BH:
                        pe.wait_ge(bspm_out, h + 1)
                        z, sp_ = PS[:, h % 5, :], BSP[:, h % 3, :]
                        mm(z[:, 0:SBW], BTRI[:, 0, :], sp_, False, True, skip_group_check=True)
                        mm(z[:, 128:256], BTRI[:, 1, :], sp_[:, 256:384], False, True, skip_group_check=True)
                        mm(z[:, 384:416], BTRI[:, 1, :], sp_[:, 416:448], False, True, skip_group_check=True) \
                            .then_inc(bs_done, 1)
                    h = s - 4
                    if h >= 0:
                        pe.wait_ge(battm_out, h + 1)
                        if h >= 4 and h % 2 == 0:
                            pe.wait_ge(bo_lo, h // 2 - 1)
                        r, c = slice(64 * (h % 2), 64 * (h % 2) + 64), slice(64 * h, 64 * h + 64)
                        out, att = PS[r, 5 + h // 2 % 2, :], BATT[:, h % 3, :]
                        mm(out[:, 0:256], BVT[:, 0, c], att[:, 0:256], True, False)
                        mm(out[:, 128:256], BVT[:, 1, c], att[:, 256:384], False, True)
                        mm(out[:, 256:288], BVP[:, c], att[:, 384:416], True, False)
                        mm(out[:, 256:288], BVT[0:TS, 2, c], att[0:TS, 416:448], False, True).then_inc(bo_done, 1)
                pe.wait_ge(bo_lo, 8)

            def mla_prep(i):
                pe.wait_ge(group_out, ST["dkv", i].g1)
                pe.wait_ge(c_in, 16 * 7)
                for b in range(2):
                    xp(PS[:, 2, b * P:(b + 1) * P], CPAST[:, b * P:(b + 1) * P])
                xp(PS[0:32, 2, 256:384], CPAST[:, CKR:CKR + CROPE])
                mm(PS[0:32, 3, 0:T], KPERM[:], CKR_[:])
                pe.wait_ge(css_out, 1)
                mm(PS[:, 0, 0:T], ONES[:], CSS[:, 0, :])
                mm(PS[:, 1, 0:T], ONES[:], CSS[:, 1, :]).then_inc(cstat_done, 1)
                pe.wait_ge(ckv_out, 1)
                pe.wait_ge(kro_out, 1)
                for tb, t0, n in TBS:
                    for b in range(2):
                        xp(PS[0:n, 4 + tb, b * P:(b + 1) * P], CKV[:, b, t0:t0 + n])
                    xp(PS[0:n, 4 + tb, 256:288], CKRO[:, t0:t0 + n]).then_inc(cxp_done, 1)
                pe.wait_ge(cxp_out, 3)

            def mla_up(i):
                st = ST["uq", i]

                def rot(g):
                    pe.wait_ge(group_out, st.g0 + g + 1)
                    for a in range(2):
                        ins = mm(PS[0:CQD, 4 * (g % 2) + 2 + a, 0:T], PERM[:], CQ96[:, 2 * g + a, :])
                    ins.then_inc(rot_done, 1)

                for g in range(8):
                    banks_free(st, g)
                    for k in range(3):
                        if g == 0 and k == 0:
                            pe.wait_ge(cq_lo, 1)
                        u = st.u0 + 3 * g + k
                        unit(u, u % SPL, g % 2, [(0, CQD), (CQD, CQD)], CQH[:, k, :], CQL[:, k, :], k == 0, k == 2)
                    if g:
                        if g >= 3:
                            pe.wait_ge(rot_out, g - 2)
                        rot(g - 1)
                pe.wait_ge(rot_out, 6)
                rot(7)
                st = ST["ukv", i]
                pe.wait_ge(ck_lo, 1)
                for t in range(4):
                    u = st.u0 + 2 * t
                    pe.wait_ge(weight_lo, u + 2)
                    pe.wait_ge(rot_out, 7)
                    banks_free(st, 2 * t)
                    S = [(u + k) % SPL for k in range(2)]
                    for a in range(4):
                        c, out = slice(P * a, P * a + 64), PS[0:64, a, 0:TK]
                        for k in range(2):
                            mm(out, WHI[:, S[k], c], CKH[:, k, :], k == 0, False)
                            mm(out, WHI[:, S[k], c], CKL[:, k, :], False, False)
                            ins = mm(out, WLO[:, S[k], c], CKH[:, k, :], False, k == 1)
                    ins.then_inc(ukv_done, 1)
                    pe.wait_ge(rot_out, 8)
                    banks_free(st, 2 * t + 1)
                    for kb, s0, n in ((0, 0, P), (1, P, P), (2, T, P), (3, TP, TS)):
                        out = PS[0:n, 4 + kb, 0:256]
                        for k in range(2):
                            wh, wl = (w[:, S[k], :].rearrange("p (h e) -> p h e", h=4)[:, :, 64:128]
                                      for w in (WHI, WLO))
                            mm(out, CKH[:, k, s0:s0 + n], wh, k == 0, False)
                            mm(out, CKL[:, k, s0:s0 + n], wh, False, False)
                            ins = mm(out, CKH[:, k, s0:s0 + n], wl, False, k == 1)
                    ins.then_inc(unit_done, 2)

            def mla_mix(i):
                pe.wait_ge(group_out, ST["ukv", i].g1)
                pe.wait_ge(crep_out, 1)
                pe.wait_ge(rot_out, 8)
                for s in range(CH + 3):
                    h = s
                    if h < CH and h % 4 == 0:
                        g = h // 4
                        if g:
                            pe.wait_ge(ss_exp, g)
                        for a in range(4):
                            q = CQ96[:, h + a, TP:T]
                            mm(PS[32 * a:32 * a + 32, 6, 0:128], q, CK96[:, h + a, T:TK])
                            ins = mm(PS[32 * a:32 * a + 32, 6, 128:160], q, CK96[:, h + a, TP:T])
                        ins.then_inc(ss_sc, 1)
                    if h < CH:
                        if h >= 2:
                            pe.wait_ge(c_exp, h - 1)
                        z = PS[:, h % 2, :]
                        mm(z[:, 0:128], CQ96[:, h, 0:128], CK96[:, h, 0:128], True, False)
                        mm(z[:, 64:128], BMROW[:, 0:128], BMROW[:, 128:192], False, True)
                        mm(z[:, 128:384], CQ96[:, h, 128:256], CK96[:, h, 0:256], True, False)
                        mm(z[:, 320:384], BMROW[:, 0:128], BMROW[:, 128:192], False, True).then_inc(cs_sc, 1)
                    if h < CH and h % 4 == 0:
                        g = h // 4
                        pe.wait_ge(ss_nrm, g + 1)
                        xp(PS[:, 7, 0:128], CPS[:, 0:128])
                        xp(PS[0:32, 7, 128:256], CPS[:, 128:160]).then_inc(ss_xp, 1)
                    h = s - 2
                    if 0 <= h < CH:
                        pe.wait_ge(c_nrm, h + 1)
                        if h >= 2:
                            pe.wait_ge(c_pt, h - 1)
                        for c in range(3):
                            ins = xp(PS[:, 2 + h % 2, P * c:P * (c + 1)], PB[:, h % 2, P * c:P * (c + 1)])
                        ins.then_inc(c_xp, 1)
                    h = s - 3
                    if h >= 0:
                        pe.wait_ge(c_pt, h + 1)
                        if h % 4 == 0:
                            pe.wait_ge(ss_pt, h // 4 + 1)
                        if h >= 4 and h % 2 == 0:
                            pe.wait_ge(c_olo, h // 2 - 1)
                        r, c = slice(64 * (h % 2), 64 * (h % 2) + 64), slice(64 * h, 64 * h + 64)
                        out, p_ = PS[r, 4 + h // 2 % 2, :], PTB[:, h % 2, :]
                        ps_ = CPTS[:, h // 4 % 2, :, 32 * (h % 4):32 * (h % 4) + 32]
                        mm(out[:, 0:256], CVT[:, 0, c], p_[:, 0:256], True, False)
                        mm(out[:, 128:256], CVT[:, 1, c], p_[:, 256:384], False, True)
                        mm(out[:, 256:288], CVT[:, 2, c], ps_[:, 0, :], True, False)
                        mm(out[:, 256:288], CVT[0:TS, 3, c], ps_[0:TS, 1, :], False, True).then_inc(c_o, 1)
                pe.wait_ge(c_olo, 8)

            for i in range(DEPTH):
                la = i // 3
                nu = 2 * i
                if i % 3 == 0:
                    xg_stage(ST["up", i], nu)
                    st = ST["qkv", i]
                    pe.wait_ge(xm_lo, 4 * la + 4)
                    pe.wait_ge(xc_lo, 4 * la + 4)
                    for x in range(12):
                        h, m = divmod(x, 3)
                        banks_free(st, x)
                        for k in range(4):
                            f = 4 * h + k + (16 if m == 2 else 0)
                            unit(st.u0 + 4 * x + k, k, x % 2, FOUR, HH[:, f, :], HL[:, f, :], k == 0, k == 3)
                    mlstm_mix(i, la)
                    hh_stage(ST["down", i], lambda k: pe.wait_ge(mh_lo, AH * la + k // 4 + 1) if k % 4 == 0 else None)
                elif i % 3 == 1:
                    xg_stage(ST["bqkv", i], nu)
                    sb_mix(i)
                    hh_stage(ST["bo", i], lambda k: None)
                else:
                    st = ST["dq", i]
                    xg_group(st, 0, 0, nu, [(P * a, P) for a in range(3)])
                    stat(nu, st.g0)
                    xg_group(ST["dkv", i], 0, 1, None, [(0, P), (P, P), (2 * P, CROPE)])
                    mla_prep(i)
                    mla_up(i)
                    mla_mix(i)
                    hh_stage(ST["co", i], lambda k: None)
                xg_stage(ST["ff1", i], nu + 1)
                st = ST["ff2", i]
                for g in range(2):
                    banks_free(st, g)

                    def chunk(j, start, stop):
                        if g == 0:
                            pe.wait_ge(h_lo, 2 * j + (8 * i + 2))
                        for k in range(8):
                            kk = 8 * j + k
                            unit(8 * j + (st.u0 + 32 * g + k), k % SPL, g, FOUR, kblock(HH, kk), kblock(HL, kk),
                                 start and k == 0, stop and k == 7)

                    chunk(0, True, False)
                    with pe.Fori(1, 3) as j:
                        chunk(j, False, False)
                    chunk(3, False, True)
            stat(2 * DEPTH, ST["ff2", DEPTH - 1].g1)
            pe.wait_ge(yf_out, 1)
            for x in range(6):
                tb, half = divmod(x, 2)
                _, t0, n = TBS[tb]
                for b in range(4):
                    ins = xp(PS[0:n, (0, 1, 2, 3, 6, 7)[x], b * P:(b + 1) * P], YF[:, 4 * half + b, t0:t0 + n])
                ins.then_inc(yo_done, 1)


_OUTS = [("y_prompt", (1, TP, D)), ("y_sample", (1, TS, D)),
         ("p_C", (2, 1, AH, ADH, ADH)), ("p_n", (2, 1, AH, ADH)), ("p_m", (2, 1, AH)), ("p_conv", (2, 1, 3, AI)),
         ("p_sb_k", (1, 1, TP, BH, BDH)), ("p_sb_v", (1, 1, TP, BH, BDH)),
         ("p_ckv", (1, 1, TP, CKR)), ("p_krope", (1, 1, TP, CROPE)),
         ("s_C", (2, 1, AH, ADH, ADH)), ("s_n", (2, 1, AH, ADH)), ("s_m", (2, 1, AH)), ("s_conv", (2, 1, 3, AI)),
         ("s_sb_k", (1, 1, TS, BH, BDH)), ("s_sb_v", (1, 1, TS, BH, BDH)),
         ("s_ckv", (1, 1, TS, CKR)), ("s_krope", (1, 1, TS, CROPE))]
_INS = ["x_prompt", "x_sample", "state_mlstm_C", "state_mlstm_n", "state_mlstm_m", "state_mlstm_conv",
        "cache_sb_k", "cache_sb_v", "cache_mla_ckv", "cache_mla_krope", "norm_mix", "norm_mlp", "norm_final",
        "a_w_up", "a_conv_w", "a_conv_b", "a_w_q", "a_w_k", "a_w_v", "a_w_gate", "a_b_i", "a_b_f", "a_g_head",
        "a_skip", "a_w_down", "b_w_qkv", "b_w_o", "c_w_dq", "c_g_q", "c_w_uq", "c_w_dkv", "c_g_kv", "c_w_ukv",
        "c_w_o", "w_ff1", "w_ff2"]


def _constants(np):
    f = np.float32
    row = np.arange(P)
    tri = np.where(row[:, None] >= row[None, :], -1.0, 0.0)
    c = {"const_pp": np.stack([np.eye(P), np.ones((P, P)), tri, -np.ones((P, P))])}
    sel = np.zeros((4, 4, P))
    for h in range(4):
        sel[h, h] = 1.0
    c["const_sel"] = sel
    q = np.arange(TP)
    new = (row[:, None] < TS)
    c["const_mask_sb"] = np.concatenate([row[:, None] < q[None, :], row[:, None] < q[None, :P], np.ones((P, TS)),
                                         new & (row[:, None] < q[None, :TS])], axis=1)
    c["const_mask_ml"] = np.concatenate([row[:, None] <= q[None, :], row[:, None] <= q[None, :P],
                                         new & (row[:, None] <= q[None, :TS])], axis=1)
    half = CROPE // 2
    inv = f(10000.0) ** (-np.arange(half, dtype=f) / f(half))
    pos = np.concatenate([np.arange(TP), PAST + np.arange(TS)]).astype(f)
    ang = (inv[:, None] * pos[None, :]).astype(f)
    cs = np.stack([np.tile(np.cos(ang), (2, 1)), np.tile(np.sin(ang), (2, 1))], axis=1)
    c["const_rope_k"] = cs
    full = np.zeros((CQD, 2, T))
    full[:, 0] = 1.0
    full[CNOPE:] = cs
    c["const_rope"] = full
    perm = np.zeros((CROPE, CROPE))
    for r in range(half):
        perm[r + half, r] = -1.0
        perm[r, r + half] = 1.0
    c["const_perm_k"] = perm
    pq = np.zeros((CQD, CQD))
    pq[CNOPE:, CNOPE:] = perm
    c["const_perm"] = pq
    c["const_bmrow"] = np.concatenate([np.where(row < 64, 1.0, 0.0), np.full(64, -2.0 ** 100)])[None, :]
    return {k: np.ascontiguousarray(v, dtype=f) for k, v in c.items()}


def kernel(**inputs):
    import numpy as _np
    import concourse.bacc as _bacc
    from concourse import mybir as _mybir
    from concourse.bass_utils import run_bass_kernel_spmd as _run

    nc = _bacc.Bacc("TRN2", target_bir_lowering=False, num_devices=1)
    arrays, d, o = {}, {}, {}
    given = {name: _np.ascontiguousarray(inputs[name]) for name in _INS}
    given.update(_constants(_np))
    for name, a in given.items():
        arrays[f"in_{name}_dram"] = a
        d[name] = nc.dram_tensor(f"in_{name}_dram", a.shape, _mybir.dt.from_np(a.dtype), kind="ExternalInput").ap()
    for name, shape in _OUTS:
        o[name] = nc.dram_tensor(f"out_{name}_dram", shape, _mybir.dt.float32, kind="ExternalOutput").ap()
    hybrid_trunk_kernel(nc, d, o)
    r = _run(nc, [arrays], core_ids=[0])
    return tuple(r.results[0][f"out_{name}_dram"] for name, _ in _OUTS)
```
